# Optimizing a Trainium2 kernel written in Bass

```python
import jax
import jax.numpy as jnp
from jax import lax
import numpy as np

D_MODEL = 1024
BATCH = 1
SEQ = 512
DEPTH = 1

SSM_EXPAND = 2
D_INNER = SSM_EXPAND * D_MODEL
SSM_HEAD_DIM = 64
SSM_HEADS = D_INNER // SSM_HEAD_DIM
SSM_GROUPS = 8
SSM_HPG = SSM_HEADS // SSM_GROUPS
SSM_STATE = 128
SSM_CONV = 4
SSM_CHUNK = 128
SSM_XBC = D_INNER + 2 * SSM_GROUPS * SSM_STATE
ATT_HEAD_DIM = 64
ATT_HEADS = D_MODEL // ATT_HEAD_DIM
ATT_KV_GROUPS = 4
ATT_HPG = ATT_HEADS // ATT_KV_GROUPS
D_ATT = ATT_HEADS * ATT_HEAD_DIM
CMP_LEN = 32
CMP_STRIDE = 16
CMP_HIDDEN = 256
SEL_BLOCK = 64
SEL_TOPK = 16
WINDOW = 512
Q_BLOCK = 128
ROPE_THETA = 500000.0
ROPE_DIM = ATT_HEAD_DIM // 4
MLP_HIDDEN = 4 * D_MODEL
NORM_EPS = 1e-6
NEG = -1e30
BIG = 1e30

SPLIT_SIZES = (D_INNER, SSM_XBC, SSM_HEADS, D_ATT, 6 * ATT_KV_GROUPS * ATT_HEAD_DIM, 3 * ATT_HEADS, 2 * D_MODEL)
SPLIT_POINTS = tuple(int(v) for v in np.cumsum(SPLIT_SIZES)[:-1])
IN_COLS = sum(SPLIT_SIZES)

kernel_name = 'hybrid_ssd_nsa_gated_block'

def rms_norm(x, g):
    x32 = x.astype(jnp.float32)
    y = x32 * lax.rsqrt(jnp.mean(x32 * x32, axis=-1, keepdims=True) + NORM_EPS)
    return (y * g.astype(jnp.float32)).astype(x.dtype)

def rope_partial(t, cos, sin):
    t32 = t.astype(jnp.float32)
    half = ROPE_DIM // 2
    t1 = t32[..., :half]
    t2 = t32[..., half:ROPE_DIM]
    out = jnp.concatenate([t1 * cos - t2 * sin, t2 * cos + t1 * sin, t32[..., ROPE_DIM:]], axis=-1)
    return out.astype(t.dtype)

def masked_softmax(s, m):
    p = jax.nn.softmax(jnp.where(m, s, NEG), axis=-1)
    return p * m

def causal_dwconv(u, w, b):
    c = u.shape[-1]
    out = lax.conv_general_dilated(u, w[:, None, :].astype(u.dtype), window_strides=(1,),
                                   padding=((SSM_CONV - 1, 0),),
                                   dimension_numbers=('NWC', 'WIO', 'NWC'),
                                   feature_group_count=c)
    return out + b.astype(u.dtype)

def ssd_chunked(xh, dt, a, bm, cm):
    bsz, s = xh.shape[:2]
    nc = s // SSM_CHUNK
    L = SSM_CHUNK

    def chunk(t):
        return t.reshape((bsz, nc, L) + t.shape[2:])

    xc = chunk(xh * dt[..., None])
    a_cs = jnp.cumsum(chunk(dt * a), axis=2)
    bc, cc = chunk(bm), chunk(cm)
    a_t = jnp.moveaxis(a_cs, 2, -1)
    diff = a_t[..., :, None] - a_t[..., None, :]
    tri = jnp.tril(jnp.ones((L, L), dtype=bool))
    decay = jnp.exp(jnp.where(tri, diff, -jnp.inf))
    cb = jnp.einsum('bclgn,bcsgn->bcgls', cc, bc)
    y_diag = jnp.einsum('bcgls,bcgrls,bcsgrp->bclgrp', cb, decay, xc)
    decay_states = jnp.exp(a_cs[:, :, -1:] - a_cs)
    states = jnp.einsum('bclgn,bclgr,bclgrp->bcgrpn', bc, decay_states, xc)
    a_tot = a_cs[:, :, -1]

    def step(h, inp):
        st, at = inp
        h_new = h * jnp.exp(at)[..., None, None] + st
        return h_new, h

    h0 = jnp.zeros_like(states[:, 0])
    _, prev = lax.scan(step, h0, (jnp.moveaxis(states, 1, 0), jnp.moveaxis(a_tot, 1, 0)))
    prev = jnp.moveaxis(prev, 0, 1)
    y_off = jnp.einsum('bclgn,bcgrpn,bclgr->bclgrp', cc, prev, jnp.exp(a_cs))
    return (y_diag + y_off).reshape(xh.shape)

def compress(t, pe, w1, w2):
    bsz, s, g, hd = t.shape
    ncmp = (s - CMP_LEN) // CMP_STRIDE + 1
    idx = jnp.arange(ncmp)[:, None] * CMP_STRIDE + jnp.arange(CMP_LEN)[None, :]
    blocks = t[:, idx] + pe[:, None, :].astype(t.dtype)
    blocks = jnp.transpose(blocks, (0, 1, 3, 2, 4)).reshape(bsz, ncmp, g, CMP_LEN * hd)
    return jax.nn.silu(blocks @ w1) @ w2

def nsa_sweep(q_nope, q_rot, kc, vc, ks, vs, kw, vw):
    bsz, s, g, r, hd = q_rot.shape
    ncmp = kc.shape[1]
    nsel = s // SEL_BLOCK
    topk = min(SEL_TOPK, nsel)
    nq = s // Q_BLOCK
    scale = hd ** -0.5
    cmp_end = jnp.arange(ncmp) * CMP_STRIDE + CMP_LEN - 1
    ci = jnp.arange(ncmp)[:, None]
    sj = jnp.arange(nsel)[None, :]
    overlap = ((ci * CMP_STRIDE < (sj + 1) * SEL_BLOCK) &
               (ci * CMP_STRIDE + CMP_LEN > sj * SEL_BLOCK)).astype(jnp.float32)
    ks_blk = jnp.transpose(ks.reshape(bsz, nsel, SEL_BLOCK, g, hd), (0, 3, 1, 2, 4))
    vs_blk = jnp.transpose(vs.reshape(bsz, nsel, SEL_BLOCK, g, hd), (0, 3, 1, 2, 4))
    kw_pad = jnp.pad(kw, ((0, 0), (WINDOW, 0), (0, 0), (0, 0)))
    vw_pad = jnp.pad(vw, ((0, 0), (WINDOW, 0), (0, 0), (0, 0)))
    b_ix = jnp.arange(bsz)[:, None, None, None]
    g_ix = jnp.arange(g)[None, :, None, None]
    blk = jnp.arange(nsel)

    def block_fn(qi):
        q0 = qi * Q_BLOCK
        t = q0 + jnp.arange(Q_BLOCK)
        qn = lax.dynamic_slice_in_dim(q_nope, q0, Q_BLOCK, axis=1)
        qr = lax.dynamic_slice_in_dim(q_rot, q0, Q_BLOCK, axis=1)
        s_c = jnp.einsum('bqgrd,bkgd->bgrqk', qn, kc).astype(jnp.float32) * scale
        p_c = masked_softmax(s_c, cmp_end[None, :] <= t[:, None])
        o_c = jnp.einsum('bgrqk,bkgd->bqgrd', p_c.astype(vc.dtype), vc)
        imp = jnp.einsum('bgrqk,kj->bgqj', p_c, overlap)
        cur = t // SEL_BLOCK
        valid = blk[None, :] <= cur[:, None]
        forced = valid & ((blk[None, :] == 0) | (blk[None, :] == cur[:, None]) | (blk[None, :] == cur[:, None] - 1))
        imp = jnp.where(forced, BIG, jnp.where(valid, imp, NEG))
        _, sel = lax.top_k(imp, topk)
        k_sel = ks_blk[b_ix, g_ix, sel].reshape(bsz, g, Q_BLOCK, topk * SEL_BLOCK, hd)
        v_sel = vs_blk[b_ix, g_ix, sel].reshape(bsz, g, Q_BLOCK, topk * SEL_BLOCK, hd)
        tok = (sel[..., None] * SEL_BLOCK + jnp.arange(SEL_BLOCK)).reshape(bsz, g, Q_BLOCK, topk * SEL_BLOCK)
        m_s = (tok <= t[:, None])[:, :, None]
        s_s = jnp.einsum('bqgrd,bgqkd->bgrqk', qr, k_sel).astype(jnp.float32) * scale
        p_s = masked_softmax(s_s, m_s)
        o_s = jnp.einsum('bgrqk,bgqkd->bqgrd', p_s.astype(v_sel.dtype), v_sel)
        kwb = lax.dynamic_slice_in_dim(kw_pad, q0, Q_BLOCK + WINDOW, axis=1)
        vwb = lax.dynamic_slice_in_dim(vw_pad, q0, Q_BLOCK + WINDOW, axis=1)
        kp = q0 - WINDOW + jnp.arange(Q_BLOCK + WINDOW)
        m_w = (kp[None, :] <= t[:, None]) & (kp[None, :] > t[:, None] - WINDOW) & (kp[None, :] >= 0)
        s_w = jnp.einsum('bqgrd,bkgd->bgrqk', qr, kwb).astype(jnp.float32) * scale
        p_w = masked_softmax(s_w, m_w)
        o_w = jnp.einsum('bgrqk,bkgd->bqgrd', p_w.astype(vwb.dtype), vwb)
        return o_c, o_s, o_w

    outs = lax.map(block_fn, jnp.arange(nq))

    def unblock(o):
        return jnp.moveaxis(o, 0, 1).reshape(bsz, s, g, r, hd)

    return unblock(outs[0]), unblock(outs[1]), unblock(outs[2])

def hybrid_layer(x, cos, sin, g_norm_mix, w_in, conv_w, conv_b, dt_bias, a_log, d_skip,
                 g_ssm_norm, w_ssm_branch, cmp_pe_k, cmp_pe_v, w_cmp_k1, w_cmp_k2,
                 w_cmp_v1, w_cmp_v2, w_attn_branch, w_o, g_norm_mlp, w_up, w_down):
    bsz, s, _ = x.shape
    h = rms_norm(x, g_norm_mix)
    proj = h @ w_in
    z, xbc, dt_raw, q, kv, att_g, mix_g = jnp.split(proj, SPLIT_POINTS, axis=-1)

    xbc = jax.nn.silu(causal_dwconv(xbc, conv_w, conv_b))
    xs, bm, cm = jnp.split(xbc, [D_INNER, D_INNER + SSM_GROUPS * SSM_STATE], axis=-1)
    xs = xs.reshape(bsz, s, SSM_GROUPS, SSM_HPG, SSM_HEAD_DIM)
    bm = bm.reshape(bsz, s, SSM_GROUPS, SSM_STATE)
    cm = cm.reshape(bsz, s, SSM_GROUPS, SSM_STATE)
    dt = jax.nn.softplus(dt_raw.astype(jnp.float32) + dt_bias.astype(jnp.float32))
    dt = dt.reshape(bsz, s, SSM_GROUPS, SSM_HPG)
    a = -jnp.exp(a_log.astype(jnp.float32)).reshape(SSM_GROUPS, SSM_HPG)
    y = ssd_chunked(xs, dt, a, bm, cm) + d_skip.reshape(SSM_GROUPS, SSM_HPG)[..., None] * xs
    y = y.reshape(bsz, s, D_INNER).astype(x.dtype) * jax.nn.silu(z)
    y = rms_norm(y.reshape(bsz, s, SSM_GROUPS, D_INNER // SSM_GROUPS),
                 g_ssm_norm.reshape(SSM_GROUPS, D_INNER // SSM_GROUPS)).reshape(bsz, s, D_INNER)
    y_ssm = y @ w_ssm_branch

    q = q.reshape(bsz, s, ATT_KV_GROUPS, ATT_HPG, ATT_HEAD_DIM)
    kv = kv.reshape(bsz, s, 6, ATT_KV_GROUPS, ATT_HEAD_DIM)
    k_c, v_c, k_s, v_s, k_w, v_w = (kv[:, :, i] for i in range(6))
    q_r = rope_partial(q, cos[:, :, None, None, :], sin[:, :, None, None, :])
    k_s = rope_partial(k_s, cos[:, :, None, :], sin[:, :, None, :])
    k_w = rope_partial(k_w, cos[:, :, None, :], sin[:, :, None, :])
    kc = compress(k_c, cmp_pe_k, w_cmp_k1, w_cmp_k2)
    vc = compress(v_c, cmp_pe_v, w_cmp_v1, w_cmp_v2)
    o_c, o_s, o_w = nsa_sweep(q, q_r, kc, vc, k_s, v_s, k_w, v_w)
    gate = jax.nn.sigmoid(att_g.astype(jnp.float32)).reshape(bsz, s, 3, ATT_KV_GROUPS, ATT_HPG, 1)
    o = gate[:, :, 0] * o_c + gate[:, :, 1] * o_s + gate[:, :, 2] * o_w
    y_att = o.reshape(bsz, s, D_ATT).astype(x.dtype) @ w_attn_branch

    g_ssm, g_att = jnp.split(jax.nn.sigmoid(mix_g.astype(jnp.float32)), 2, axis=-1)
    mixed = (g_ssm * y_ssm + g_att * y_att).astype(x.dtype)
    x = x + mixed @ w_o

    h = rms_norm(x, g_norm_mlp)
    x = x + jnp.square(jax.nn.relu(h @ w_up)) @ w_down
    return x

def setup_inputs(seed: int = 0) -> dict:
    key = jax.random.key(seed)
    ks = jax.random.split(key, 24)
    f32 = jnp.float32

    def nrm(k, shape, fan_in):
        return jax.random.normal(k, shape, f32) * (fan_in ** -0.5)

    def gain(k, shape):
        return 1.0 + 0.02 * jax.random.normal(k, shape, f32)

    x = jax.random.normal(ks[0], (BATCH, SEQ, D_MODEL), f32)
    positions = jnp.broadcast_to(jnp.arange(SEQ, dtype=jnp.int32), (BATCH, SEQ)).astype(jnp.int32)
    dt0 = jnp.exp(jax.random.uniform(ks[6], (DEPTH, SSM_HEADS), f32) * (jnp.log(0.1) - jnp.log(0.001)) + jnp.log(0.001))
    dt_bias = dt0 + jnp.log(-jnp.expm1(-dt0))
    a_log = jnp.log(jax.random.uniform(ks[7], (DEPTH, SSM_HEADS), f32, 1.0, 16.0))
    return {
        'x': x,
        'positions': positions,
        'g_norm_mix': gain(ks[1], (DEPTH, D_MODEL)),
        'w_in': nrm(ks[2], (DEPTH, D_MODEL, IN_COLS), D_MODEL),
        'conv_w': nrm(ks[3], (DEPTH, SSM_CONV, SSM_XBC), SSM_CONV),
        'conv_b': 0.02 * jax.random.normal(ks[4], (DEPTH, SSM_XBC), f32),
        'dt_bias': dt_bias,
        'a_log': a_log,
        'd_skip': 1.0 + 0.1 * jax.random.normal(ks[5], (DEPTH, SSM_HEADS), f32),
        'g_ssm_norm': gain(ks[8], (DEPTH, D_INNER)),
        'w_ssm_branch': nrm(ks[9], (DEPTH, D_INNER, D_MODEL), D_INNER),
        'cmp_pe_k': 0.1 * jax.random.normal(ks[10], (DEPTH, CMP_LEN, ATT_HEAD_DIM), f32),
        'cmp_pe_v': 0.1 * jax.random.normal(ks[11], (DEPTH, CMP_LEN, ATT_HEAD_DIM), f32),
        'w_cmp_k1': nrm(ks[12], (DEPTH, CMP_LEN * ATT_HEAD_DIM, CMP_HIDDEN), CMP_LEN * ATT_HEAD_DIM),
        'w_cmp_k2': nrm(ks[13], (DEPTH, CMP_HIDDEN, ATT_HEAD_DIM), CMP_HIDDEN),
        'w_cmp_v1': nrm(ks[14], (DEPTH, CMP_LEN * ATT_HEAD_DIM, CMP_HIDDEN), CMP_LEN * ATT_HEAD_DIM),
        'w_cmp_v2': nrm(ks[15], (DEPTH, CMP_HIDDEN, ATT_HEAD_DIM), CMP_HIDDEN),
        'w_attn_branch': nrm(ks[16], (DEPTH, D_ATT, D_MODEL), D_ATT),
        'w_o': nrm(ks[17], (DEPTH, D_MODEL, D_MODEL), D_MODEL),
        'g_norm_mlp': gain(ks[18], (DEPTH, D_MODEL)),
        'w_up': nrm(ks[19], (DEPTH, D_MODEL, MLP_HIDDEN), D_MODEL),
        'w_down': nrm(ks[20], (DEPTH, MLP_HIDDEN, D_MODEL), MLP_HIDDEN),
        'g_norm_final': gain(ks[21], (D_MODEL,)),
    }

def reference(x, positions, g_norm_mix, w_in, conv_w, conv_b, dt_bias, a_log, d_skip,
              g_ssm_norm, w_ssm_branch, cmp_pe_k, cmp_pe_v, w_cmp_k1, w_cmp_k2,
              w_cmp_v1, w_cmp_v2, w_attn_branch, w_o, g_norm_mlp, w_up, w_down, g_norm_final):
    inv_freq = ROPE_THETA ** (-jnp.arange(0, ROPE_DIM, 2, dtype=jnp.float32) / ROPE_DIM)
    ang = positions.astype(jnp.float32)[..., None] * inv_freq
    cos, sin = jnp.cos(ang), jnp.sin(ang)
    for l in range(DEPTH):
        x = hybrid_layer(x, cos, sin, g_norm_mix[l], w_in[l], conv_w[l], conv_b[l], dt_bias[l],
                         a_log[l], d_skip[l], g_ssm_norm[l], w_ssm_branch[l], cmp_pe_k[l],
                         cmp_pe_v[l], w_cmp_k1[l], w_cmp_k2[l], w_cmp_v1[l], w_cmp_v2[l],
                         w_attn_branch[l], w_o[l], g_norm_mlp[l], w_up[l], w_down[l])
    return rms_norm(x, g_norm_final)


_drawn_inputs = setup_inputs


def setup_inputs(seed=0):
    import zlib

    import numpy as np

    out = dict(_drawn_inputs(seed))
    spreads = {}
    factors = {'g_norm_mix': 3.227,
     'conv_b': 3.818,
     'g_ssm_norm': 16.019,
     'cmp_pe_k': 8.0,
     'cmp_pe_v': 19.871,
     'g_norm_mlp': 10.525,
     'g_norm_final': 21.135,
     'd_skip': 39.887}
    for name, (base, spread) in spreads.items():
        noise = np.random.default_rng([zlib.crc32(name.encode()), seed]).standard_normal(out[name].shape)
        drawn = base * np.exp(spread * noise) if base else spread * noise
        out[name] = jnp.asarray(drawn.astype(out[name].dtype))
    for name, factor in factors.items():
        out[name] = (out[name] * factor).astype(out[name].dtype)
    return out
```

```python
from contextlib import ExitStack

import numpy as np

import concourse.bass as bass
from concourse import mybir

F32 = mybir.dt.float32
F32R = mybir.dt.float32r
BF16 = mybir.dt.bfloat16
I32 = mybir.dt.int32
ALU = mybir.AluOpType
ACT = mybir.ActivationFunctionType
AX = mybir.AxisListType

P = 128
S = 512
D = 1024
KT = D // P
NC = S // P
D_INNER = 2048
HEADS = 32
GROUPS = 8
HPG = HEADS // GROUPS
N_STATE = 128
XBC = D_INNER + 2 * GROUPS * N_STATE
CONV = 4
HD = 64
A_HEADS = 16
KVG = 4
R = A_HEADS // KVG
CMP = (S - 32) // 16 + 1
CMP_HID = 256
HIDDEN = 4 * D
EPS = 1e-6
NEG = -1e30

C_Z = 0
C_XS = D_INNER
C_B = C_XS + D_INNER
C_C = C_B + GROUPS * N_STATE
C_DT = C_XS + XBC
C_Q = C_DT + HEADS
C_KV = C_Q + A_HEADS * HD
C_AG = C_KV + 6 * KVG * HD
C_MIX = C_AG + 3 * A_HEADS

U_SMALL = 0
U_KV = 2
U_Q = U_KV + 12
U_SSM = U_Q + 8
U_MIX = U_SSM + 6 * GROUPS
U_WO = U_MIX + 40
U_MLP = U_WO + 8
UNITS = U_MLP + 64

K_ID, K_TRI, K_STRI, K_PERM, K_CB, K_CM, K_F = 0, 128, 256, 384, 512, 640, 768
K_HALF = 770
K_N = 770 + 128

MAGIC = 12582912.0
TWO_PI = 2 * np.pi
PI_A = 6.28125
PI_B = float(np.float32(np.round((TWO_PI - PI_A) * 2**20) / 2**20))
PI_C = float(TWO_PI - PI_A - PI_B)
SIN_MAX = 3.1415925


def shape_constants():
    c = np.zeros((P, K_N), np.float32)
    i = np.arange(P)[:, None]
    j = np.arange(P)[None, :]
    c[:, K_ID:K_ID + P] = i == j
    c[:, K_TRI:K_TRI + P] = i <= j
    c[:, K_STRI:K_STRI + P] = i > j
    d = np.arange(P) % HD
    partner = np.where(d < 8, np.arange(P) + 8, np.arange(P) - 8)
    rot = d < 16
    for p in range(P):
        if rot[p]:
            c[partner[p], K_PERM + p] = 1.0
    c[:, K_CB:K_CB + P] = np.where(j <= i, 0.0, NEG)
    for t in range(NC):
        k = np.arange(32)[None, :]
        c[:, K_CM + 32 * t:K_CM + 32 * t + 32] = (16 * k + 31 <= P * t + i) & (k < CMP)
    inv = (np.float32(500000.0) ** (-np.arange(0, 16, 2, dtype=np.float32) / np.float32(16))).astype(np.float32)
    c[:, K_F] = np.where(rot, inv[d % 8], 0.0)
    c[:, K_F + 1] = np.where(rot, np.where(d < 8, -1.0, 1.0), 0.0)
    c[0, K_HALF:K_HALF + HD] = 1.0
    c[1, K_HALF + HD:K_HALF + P] = 1.0
    return c


class Steps:

    def __init__(self, eng, sem):
        self.eng, self.sem, self.n, self.base = eng, sem, 0, 0

    def __call__(self, ins):
        ins.then_inc(self.sem, 1)
        self.n += 1

    def wait(self):
        self.eng.wait_ge(self.sem, self.base + self.n)

    def loop(self, it, per):
        self.before, self.per = self.n, per
        self.base, self.n = self.before + it * per, 0

    def end(self, rounds):
        assert self.n == self.per, (self.n, self.per)
        self.base, self.n = 0, self.before + rounds * self.per


def build(nc, a, out):
    ctx = ExitStack()
    with ctx:
        sem_names = {}

        def sem(name):
            return ctx.enter_context(nc.semaphore(name))

        at = [16512]

        def sb(name, shape, dt=F32, offset=None):
            size = 4 if dt in (F32, F32R, I32) else 2
            nbytes = (int(np.prod(shape[1:])) * size + 31) // 32 * 32
            where = at[0] if offset is None else offset
            if offset is None:
                at[0] += nbytes
            assert where + nbytes <= 229344, (name, where + nbytes)
            return nc.alloc_sbuf_tensor_at(name, list(shape), dt, offset=where)

        cst = sb("cst", [P, K_N])
        ident = cst[:, K_ID:K_ID + P]
        tri = cst[:, K_TRI:K_TRI + P]
        stri = cst[:, K_STRI:K_STRI + P]
        perm = cst[:, K_PERM:K_PERM + P]
        cmask = cst[:, K_CM:K_CM + 128].rearrange("p (t k) -> p t k", t=NC)
        ones = sb("ones", [P, P])
        mean_ssm = sb("mean_ssm", [P, P])
        ident_bf = sb("ident_bf", [P, P], BF16)
        causal_bf = sb("causal_bf", [P, P], BF16)
        vt = sb("vt", [P, 240])
        eps_col = sb("eps_col", [P, 8])
        stat = sb("stat", [P, 16])
        gate = sb("gate", [P, NC, 48])
        dtT = sb("dtT", [P, 2, NC, HEADS])
        decs = sb("decs", [P, 2, NC, HEADS])
        dd = sb("dd", [P, NC, HEADS])
        raw = [sb(f"raw{i}", [P, KT * P]) for i in range(2)]
        whi = [sb(f"whi{i}", [P, KT * P], F32R) for i in range(2)]
        wlo = [sb(f"wlo{i}", [P, KT * P], F32R) for i in range(2)]
        h_hi = sb("h_hi", [P, KT, S], F32R)
        h_lo = sb("h_lo", [P, KT, S], F32R)
        o_hi = sb("o_hi", [P, KT, S], F32R)
        o_lo = sb("o_lo", [P, KT, S], F32R)
        region = at[0]

        x_sb = sb("x_sb", [P, NC, D])
        xn = sb("xn", [P, NC, D])
        sq_junk = sb("sq_junk", [P, D])
        dtw = sb("dtw", [HEADS, 8, S])
        rows1 = sb("rows1", [P, P])
        rows2 = sb("rows2", [96, P])
        small = sb("small", [HEADS, 4])
        d_two = sb("d_two", [2, HEADS // 2])
        ag = sb("ag", [48, S])
        at[0] = region
        kcx = sb("kcx", [P, 2, KVG, S])
        kT = sb("kT", [P, 2, 2, S])
        vtok = sb("vtok", [P, 2, NC, KVG * HD])
        assert at[0] <= region + 2 * 4 * NC * D
        at[0] = region + 2 * 4 * NC * D + 4 * D + 8 * 4 * S + 3 * 4 * S
        w1c = sb("w1c", [P, 2, 16, CMP_HID], offset=at[0] - 0)
        at[0] += 32768
        w2c = sb("w2c", [P, 2, 2, 2, HD])
        ropeC = sb("ropeC", [P, S])
        ropeS = sb("ropeS", [P, S])
        pos_i = sb("pos_i", [P, S], I32)
        rt_at = at[0]
        rt = sb("rt", [P, 3, S])
        cs = sb("cs", [P, 2, NC, 4, 32], offset=rt_at)
        vtmp = sb("vtmp", [P, 2, S])
        cmp_end = at[0]
        at[0] = region + 2 * 4 * NC * D
        blk = sb("blk", [P, 16, P])
        hid = sb("hid", [P, 2, 2, KVG, 32])
        hidr = sb("hidr", [P, 2, KVG, 4, 32])
        kc = sb("kc", [P, KVG, 32])
        vc = sb("vc", [P, KVG, HD])
        cbias = sb("cbias", [P, NC, 32])
        rtmp = sb("rtmp", [P, S])
        assert at[0] <= region + 2 * 4 * NC * D + 4 * D + 8 * 4 * S
        at[0] = region + 2 * 4 * NC * D + 4 * D + 8 * 4 * S + 3 * 4 * S
        q_s = sb("q_s", [P, 4, S])
        q_r = sb("q_r", [P, 4, S])
        prob = [sb(f"prob{i}", [P, S]) for i in range(3)]
        pT = [sb(f"pT{i}", [P, S]) for i in range(2)]
        cp = sb("cp", [P, 3, 8, 32])
        pcT = [sb(f"pcT{i}", [P, 2, P]) for i in range(2)]
        nmax = sb("nmax", [P, 4])
        esum = sb("esum", [P, 4])
        rsum = sb("rsum", [P, 4])
        cst8 = sb("cst8", [P, 4, 8])
        assert at[0] <= region + 2 * 4 * NC * D + 4 * D + 8 * 4 * S + 3 * 4 * S + 32768

        at[0] = region
        y_hi = sb("y_hi", [P, 2 * KT, S], F32R)
        y_lo = sb("y_lo", [P, 2 * KT, S], F32R)
        after_y = at[0]
        grp = sb("grp", [P, 6, S])
        xdt = sb("xdt", [P, NC, HPG * HD])
        xdd_at = at[0]
        xdd = sb("xdd", [P, NC - 1, HPG * HD])
        btok = sb("btok", [P, NC, N_STATE])
        cbm = sb("cbm", [P, NC, P])
        segr = sb("segr", [P, 2, HPG, P])
        mdec = sb("mdec", [P, NC, HPG, P])
        prev = sb("prev", [P, NC - 1, HPG * HD])
        dtab = sb("dtab", [P, NC - 1, HPG * HD])
        yt = sb("yt", [P, 2, S])
        eo = sb("eo", [P, 2, (NC - 1) * P], offset=xdd_at)
        ssm_end = at[0]
        sq = segr[:].rearrange("p a h l -> p a (h l)")
        rs = mdec[:, 0].rearrange("p h l -> p (h l)")
        yn = mdec[:, 1:3].rearrange("p c h l -> p c (h l)")
        at[0] = after_y
        m_hi = sb("m_hi", [P, KT, S], F32R)
        m_lo = sb("m_lo", [P, KT, S], F32R)
        sig = sb("sig", [P, 2, S])
        mt = sb("mt", [P, 2, S])
        at[0] = region
        x1 = sb("x1", [P, NC, D])
        xn2 = sb("xn2", [P, NC, D])
        u_hi = sb("u_hi", [P, KT, S], F32R)
        u_lo = sb("u_lo", [P, KT, S], F32R)
        assert at[0] <= after_y
        at[0] = after_y
        gfin = sb("gfin", [P, D])
        rel = sb("rel", [P, 2, S])
        uf = sb("uf", [P, 2, S])
        junk2 = sb("junk2", [P, D])
        stat2 = sb("stat2", [P, 2, 16])

        V_CW, V_CB, V_GMIX, V_GSSM, V_GMLP, V_PE, V_D = 0, 128, 160, 168, 184, 192, 224

        bank = [ctx.enter_context(nc.psum_tensor(f"bank{i}", [P, 512], F32)) for i in range(8)]

        raw_loaded = [sem(f"raw_loaded{i}") for i in range(2)]
        whi_ready = sem("whi_ready")
        wlo_ready = sem("wlo_ready")
        unit_done = sem("unit_done")
        unit_read = [sem(f"unit_read{i}") for i in range(2)]
        const_loaded = sem("const_loaded")
        x_loaded = [sem(f"x_loaded{i}") for i in range(NC)]
        rows_loaded = sem("rows_loaded")
        small_loaded = sem("small_loaded")
        cmpw_loaded = sem("cmpw_loaded")
        ones_set = sem("ones_set")
        vec_turned = sem("vec_turned")
        vec_ready = sem("vec_ready")
        sumsq_ready = sem("sumsq_ready")
        ms_ready = sem("ms_ready")
        rms_ready = sem("rms_ready")
        rstd_ready = sem("rstd_ready")
        xn_ready = sem("xn_ready")
        xn_turned = sem("xn_turned")
        hhi_ready = sem("hhi_ready")
        hlo_ready = sem("hlo_ready")
        masks_ready = sem("masks_ready")
        dve_steps = sem("dve_steps")
        dt_neg = sem("dt_neg")
        dt_exp = sem("dt_exp")
        dt_one = sem("dt_one")
        dt_log = sem("dt_log")
        dt_ready = sem("dt_ready")
        dt_turned = sem("dt_turned")
        dtT_ready = sem("dtT_ready")
        dec_summed = sem("dec_summed")
        dec_ready = sem("dec_ready")
        ag_ready = sem("ag_ready")
        ag_turned = sem("ag_turned")
        gate_ready = sem("gate_ready")
        angle_ready = sem("angle_ready")
        sin_ready = sem("sin_ready")
        rope_ready = sem("rope_ready")
        k_copied = sem("k_copied")
        k_swapped = sem("k_swapped")
        k_ready = sem("k_ready")
        v_copied = sem("v_copied")
        v_turned = sem("v_turned")
        v_ready = sem("v_ready")
        kcx_ready = sem("kcx_ready")
        blk_ready = sem("blk_ready")
        hid_summed = sem("hid_summed")
        hid_ready = sem("hid_ready")
        hid_zeroed = sem("hid_zeroed")
        hidr_ready = sem("hidr_ready")
        kvc_summed = sem("kvc_summed")
        kvc_ready = sem("kvc_ready")
        q_copied = sem("q_copied")
        q_swapped = sem("q_swapped")
        q_ready = sem("q_ready")
        cs_ready = sem("cs_ready")
        cs_read = sem("cs_read")
        cs_centred = sem("cs_centred")
        cs_exp = sem("cs_exp")
        cp_ready = sem("cp_ready")
        cp_turned = sem("cp_turned")
        pcT_ready = sem("pcT_ready")
        s_ready = sem("s_ready")
        max_ready = sem("max_ready")
        exp_ready = sem("exp_ready")
        prob_ready = sem("prob_ready")
        prob_turned = sem("prob_turned")
        pT_ready = sem("pT_ready")
        pv_done = sem("pv_done")
        ohi_ready = sem("ohi_ready")
        olo_ready = sem("olo_ready")

        segr_ready = sem("segr_ready")
        seg_summed = sem("seg_summed")
        dec_exp = sem("dec_exp")
        dtab_ready = sem("dtab_ready")
        conv_begun = sem("conv_begun")
        conv_step = sem("conv_step")
        conv_summed = sem("conv_summed")
        conv_ready = sem("conv_ready")
        z_ready = sem("z_ready")
        x_turned = sem("x_turned")
        b_turned = sem("b_turned")
        btok_ready = sem("btok_ready")
        cb_done = sem("cb_done")
        cbm_ready = sem("cbm_ready")
        xdt_ready = sem("xdt_ready")
        xdd_ready = sem("xdd_ready")
        mdec_ready = sem("mdec_ready")
        st_done = sem("st_done")
        prev_ready = sem("prev_ready")
        yd_done = sem("yd_done")
        eo_summed = sem("eo_summed")
        eo_ready = sem("eo_ready")
        yo_done = sem("yo_done")
        y_gated = sem("y_gated")
        ysq_ready = sem("ysq_ready")
        yms_done = sem("yms_done")
        yln_ready = sem("yln_ready")
        yrs_ready = sem("yrs_ready")
        yn_ready = sem("yn_ready")
        yhi_ready = sem("yhi_ready")
        ylo_ready = sem("ylo_ready")
        ssm_steps = sem("ssm_steps")
        mix_sig = sem("mix_sig")
        mix_sum = sem("mix_sum")
        mix_part = sem("mix_part")
        mhi_ready = sem("mhi_ready")
        mlo_ready = sem("mlo_ready")
        x1_loaded = sem("x1_loaded")
        gfin_loaded = sem("gfin_loaded")
        x1_ready = sem("x1_ready")
        n2_sumsq = [sem(f"n2_sumsq{i}") for i in range(2)]
        n2_ms = [sem(f"n2_ms{i}") for i in range(2)]
        n2_rms = [sem(f"n2_rms{i}") for i in range(2)]
        n2_rstd = [sem(f"n2_rstd{i}") for i in range(2)]
        xn2_ready = sem("xn2_ready")
        xn2_turned = sem("xn2_turned")
        h2hi_ready = sem("h2hi_ready")
        h2lo_ready = sem("h2lo_ready")
        relu_ready = sem("relu_ready")
        uf_ready = sem("uf_ready")
        uhi_ready = sem("uhi_ready")
        ulo_ready = sem("ulo_ready")
        down_added = sem("down_added")
        out_ready = sem("out_ready")
        out_stored = sem("out_stored")

        w_in = a["w_in"][0]

        def columns(weight, row0, col, width=P):
            return weight[row0:row0 + D, bass.ds(col, width)].rearrange("(k p) n -> p k n", p=P)

        block = ctx.enter_context(nc.Block())

        @block.sync
        def _(sp):
            sp.dma_start(cst[:], a["consts"]).then_inc(const_loaded, 16)
            for c in range(NC):
                sp.dma_start(x_sb[:, c, :], a["x"][0, c * P:(c + 1) * P, :]).then_inc(x_loaded[c], 16)
            sp.dma_start(rows1[:], a["conv_w"][0].rearrange("k (t p) -> (k t) p", p=P)).then_inc(rows_loaded, 16)
            at_row = 0
            for name in ("conv_b", "g_norm_mix", "g_ssm_norm", "g_norm_mlp"):
                n = a[name].shape[1] // P
                sp.dma_start(rows2[at_row:at_row + n, :],
                             a[name][0].rearrange("(t p) -> t p", p=P)).then_inc(rows_loaded, 16)
                at_row += n
            for name in ("cmp_pe_k", "cmp_pe_v"):
                sp.dma_start(rows2[at_row:at_row + 16, :],
                             a[name][0].rearrange("(j e) d -> j (e d)", e=2)).then_inc(rows_loaded, 16)
                at_row += 16
            with nc.allow_non_contiguous_dma(reason="a few small vectors"):
                sp.dma_start(small[:, 0:1], a["dt_bias"].rearrange("a h -> h a")).then_inc(small_loaded, 16)
                sp.dma_start(small[:, 1:2], a["a_log"].rearrange("a h -> h a")).then_inc(small_loaded, 16)
                sp.dma_start(d_two[:], a["d_skip"][0].rearrange("(t e) -> e t", e=2)).then_inc(small_loaded, 16)
            sp.dma_start(pos_i[:], a["positions"].to_broadcast([P, S])).then_inc(small_loaded, 16)

            def load(u, slot, source):
                if not (isinstance(u, int) and u < 2):
                    sp.wait_ge(wlo_ready, u - 1)
                dst = raw[slot][:].rearrange("p (k n) -> p k n", k=source.shape[1])
                sp.dma_start(dst, source).then_inc(raw_loaded[slot], 16)

            load(0, 0, columns(w_in, 0, C_DT))
            load(1, 1, columns(w_in, 0, C_AG))
            for j in range(12):
                load(U_KV + j, j % 2, columns(w_in, 0, C_KV + P * j))
                if j == 1:
                    for i, name in enumerate(("w_cmp_k1", "w_cmp_v1")):
                        sp.dma_start(w1c[:, i], a[name][0].rearrange("(j p) n -> p j n", p=P)).then_inc(cmpw_loaded, 16)
                    for i, name in enumerate(("w_cmp_k2", "w_cmp_v2")):
                        for e in range(2):
                            sp.dma_start(w2c[:, i, :, e, :],
                                         a[name][0].rearrange("(j p) n -> p j n", p=P)).then_inc(cmpw_loaded, 16)

            with sp.Fori(0, 2) as rr:
                for j in range(4):
                    pp, r2 = divmod(j, 2)
                    u = rr * 4 + (U_Q + j)
                    sp.wait_ge(wlo_ready, u - 1)
                    dst = raw[j % 2][:].rearrange("p (k e n) -> p k e n", k=KT, e=2)
                    for e in range(2):
                        head = rr * 2 + ((2 * pp + e) * R + r2)
                        sp.dma_start(dst[:, :, e, :], columns(w_in, 0, head * HD + C_Q, HD)).then_inc(raw_loaded[j % 2], 16)

            with sp.Fori(1, GROUPS + 1) as after:
                for j, (width, col) in enumerate(((256, C_XS), (256, C_XS + P), (P, C_B), (P, C_C),
                                                  (256, C_Z), (256, C_Z + P))):
                    load(after * 6 + (U_SSM - 6 + j), j % 2, columns(w_in, 0, after * width + (col - width)))
            with sp.Fori(0, 4) as m:
                for t in range(2):
                    col = m * 256 + t * P
                    for i, (weight, row0, c0) in enumerate(((a["w_ssm_branch"][0], 0, 0), (a["w_ssm_branch"][0], D, 0),
                                                            (w_in, 0, C_MIX), (a["w_attn_branch"][0], 0, 0),
                                                            (w_in, 0, C_MIX + D))):
                        j = 5 * t + i
                        load(m * 10 + (U_MIX + j), j % 2, columns(weight, row0, col + c0))

            def rows(weight, row, half):
                return weight[bass.ds(row, 2 * P), half * 512:(half + 1) * 512].rearrange("(k p) n -> p k n", p=P)

            for j in range(8):
                load(U_WO + j, j % 2, rows(a["w_o"][0], (j % 4) * 2 * P, j // 4))
                if j == 2:
                    sp.wait_ge(unit_done, U_WO)
                    sp.dma_start(x1[:], a["x"][0].rearrange("(c p) n -> p c n", p=P)).then_inc(x1_loaded, 16)
            with sp.Fori(0, 4) as q:
                for j in range(8):
                    load(q * 16 + (U_MLP + j), j % 2, columns(a["w_up"][0], 0, q * D + j * P))
                for j in range(8):
                    load(q * 16 + (U_MLP + 8 + j), j % 2, rows(a["w_down"][0], q * D + (j % 4) * 2 * P, j // 4))
            sp.wait_ge(unit_done, U_MLP)
            sp.dma_start(gfin[:], a["g_norm_final"].rearrange("(a n) -> a n", a=1).to_broadcast([P, D])).then_inc(gfin_loaded, 16)
            for c in range(NC):
                sp.wait_ge(out_ready, c + 1)
                sp.dma_start(out[0, c * P:(c + 1) * P, :], xn2[:, c, :]).then_inc(out_stored, 16)
            sp.wait_ge(out_stored, 16 * NC)

        def loaded(u):
            return 16 * (u // 2 + 1)

        KV_LANDED = loaded(U_Q - 1)
        SSM_LANDED = KV_LANDED + 128 + 16
        MIX_LANDED = SSM_LANDED + 16 * 3 * GROUPS
        WO_LANDED = MIX_LANDED + 16 * 20
        MLP_LANDED = WO_LANDED + 16 * 4
        Z_READ = U_Q // 2 + 1

        @block.gpsimd
        def _(pool):
            nc.gpsimd.memset(ones[:], 1.0).then_inc(ones_set, 1)
            nc.gpsimd.memset(mean_ssm[:], GROUPS / D_INNER).then_inc(ones_set, 1)
            nc.gpsimd.memset(eps_col[:], EPS).then_inc(ones_set, 1)
            with pool.Fori(0, UNITS // 2) as pair:
                for slot in range(2):
                    pool.wait_ge(whi_ready, pair * 2 + (slot + 1))
                    nc.gpsimd.tensor_tensor(wlo[slot][:], raw[slot][:], whi[slot][:].bitcast(F32),
                                            ALU.subtract).then_inc(wlo_ready, 1)

        @block.scalar
        def _(act):
            def split(u, slot, landed):
                act.wait_ge(raw_loaded[slot], landed)
                if not (isinstance(u, int) and u < 2):
                    act.wait_ge(unit_done, u - 1)
                nc.scalar.activation(whi[slot][:], raw[slot][:], ACT.Copy).then_inc(whi_ready, 1)

            def norm_squares(src, loads):
                for c in range(NC):
                    act.wait_ge(loads[c], 16)
                    if c:
                        act.wait_ge(sumsq_ready, c)
                    nc.scalar.activation(sq_junk[:], src[:, c, :], ACT.Square,
                                         accum_out=stat[:, c:c + 1]).then_inc(sumsq_ready, 1)
                act.wait_ge(ms_ready, 1)
                nc.scalar.activation(stat[:, 8:12], stat[:, 4:8], ACT.Sqrt).then_inc(rms_ready, 1)

            norm_squares(x_sb, x_loaded)
            split(0, 0, 16)
            split(1, 1, 16)
            act.wait_ge(vec_ready, 1)
            for k in range(KT):
                act.wait_ge(xn_turned, k + 1)
                nc.scalar.activation(h_hi[:, k, :], bank[3 + k % 4][:], ACT.Copy,
                                     scale=vt[:, V_GMIX + k:V_GMIX + k + 1]).then_inc(hhi_ready, 1)
            act.wait_ge(angle_ready, 1)
            nc.scalar.activation(ropeS[:], rt[:, 0, :], ACT.Sin).then_inc(sin_ready, 1)
            act.wait_ge(angle_ready, 2)
            nc.scalar.activation(ropeC[:], rt[:, 1, :], ACT.Sin).then_inc(sin_ready, 1)
            act.wait_ge(unit_done, 1)
            split(2, 0, loaded(2))
            act.wait_ge(small_loaded, 64)
            nc.scalar.activation(small[:, 2:3], small[:, 1:2], ACT.Exp).then_inc(dt_exp, 1)
            act.wait_ge(dt_neg, 1)
            nc.scalar.activation(dtw[:, 2, :], dtw[:, 1, :], ACT.Exp).then_inc(dt_exp, 1)
            act.wait_ge(dt_one, 1)
            nc.scalar.activation(dtw[:, 4, :], dtw[:, 3, :], ACT.Ln).then_inc(dt_log, 1)
            split(3, 1, loaded(3))
            nc.scalar.activation(ag[:], bank[1][0:48, :], ACT.Sigmoid).then_inc(unit_read[1], 1)
            for j in range(12):
                u = U_KV + j
                if j < 10:
                    split(u + 2, j % 2, loaded(u + 2))
                else:
                    split(u + 2, j % 2, KV_LANDED + 32)
                kind, pp = divmod(j, 2)
                if kind in (3, 5):
                    b = kind // 4
                    act.wait_ge(unit_done, u + 1)
                    if b or pp:
                        act.wait_ge(v_turned, 2 * b + pp)
                    nc.scalar.activation(vtmp[:, pp, :], bank[u % 2][:], ACT.Copy).then_inc(unit_read[u % 2], 1)
                    act.wait_ge(v_turned, 2 * b + pp + 1)
                    nc.scalar.activation(vtok[:, b, :, pp * P:(pp + 1) * P],
                                         bank[4 + pp][:].rearrange("p (c n) -> p c n", c=NC),
                                         ACT.Copy).then_inc(v_ready, 1)
                if j == 4:
                    act.wait_ge(dec_summed, 1)
                    nc.scalar.activation(decs[:].rearrange("p a c h -> p (a c h)"), bank[3][:, 0:256],
                                         ACT.Exp).then_inc(dec_ready, 1)
            for i in range(2):
                act.wait_ge(hid_summed, i + 1)
                act.wait_ge(hid_zeroed, 1)
                nc.scalar.activation(hid[:, i, :, :, 0:CMP],
                                     bank[2 + i][:, 0:256].rearrange("p (h g k) -> p h g k", h=2, k=32)[:, :, :, 0:CMP],
                                     ACT.Silu).then_inc(hid_ready, 1)

            with act.Fori(0, 2) as rr:
                for j in range(4):
                    act.wait_ge(unit_done, rr * 4 + (U_Q + j + 1))
                    act.wait_ge(raw_loaded[j % 2], rr * 64 + (KV_LANDED + 64) if j < 2 else rr * 48 + (KV_LANDED + 96))
                    nc.scalar.activation(whi[j % 2][:], raw[j % 2][:], ACT.Copy).then_inc(whi_ready, 1)
                    nc.scalar.activation(q_s[:, j, :], bank[j % 2][:], ACT.Copy,
                                         scale=float(HD) ** -0.5).then_inc(q_copied, 1)

                def cmp_exp(i):
                    act.wait_ge(cs_centred, rr * NC + (i + 1))
                    nc.scalar.activation(cp[:, 1], cp[:, 0], ACT.Exp).then_inc(cs_exp, 1)

                def exp(n):
                    act.wait_ge(max_ready, rr * 64 + (n + 1))
                    if n >= 3:
                        act.wait_ge(prob_turned, rr * 64 + (n - 2))
                    w = (n // 16 + 1) * P
                    nc.scalar.activation(prob[n % 3][:, 0:w], bank[1 + n % 3][:, 0:w], ACT.Exp,
                                         bias=nmax[:, n % 4:n % 4 + 1],
                                         accum_out=esum[:, n % 4:n % 4 + 1]).then_inc(exp_ready, 1)

                def high_out(g4):
                    i, g = divmod(g4, KVG)
                    act.wait_ge(pv_done, rr * 64 + (4 * g4 + 4))
                    nc.scalar.activation(o_hi[:, bass.ds(rr + 2 * g, 1), i * P:(i + 1) * P],
                                         bank[6 + g % 2][:, 0:P], ACT.Copy).then_inc(ohi_ready, 1)

                def copy_cmp(i):
                    act.wait_ge(cp_turned, rr * NC + (i + 1))
                    nc.scalar.activation(pcT[i % 2][:].rearrange("p t q -> p (t q)"), bank[0][:, 0:2 * P],
                                         ACT.Copy).then_inc(pcT_ready, 1)

                cmp_exp(0)
                exp(0)
                exp(1)
                copy_cmp(0)
                for n in range(64):
                    w = (n // 16 + 1) * P
                    act.wait_ge(prob_turned, rr * 64 + (n + 1))
                    if n >= 2:
                        act.wait_ge(pv_done, rr * 64 + (n - 1))
                    nc.scalar.activation(pT[n % 2][:, 0:w], bank[4 + n % 2][:, 0:w], ACT.Copy).then_inc(pT_ready, 1)
                    if n + 2 < 64:
                        exp(n + 2)
                    if n % 16 == 6 and n < 48:
                        cmp_exp(n // 16 + 1)
                    if n % 16 == 12 and n < 48:
                        copy_cmp(n // 16 + 1)
                    if n % 4 == 1 and n > 4:
                        high_out(n // 4 - 1)
                high_out(15)

            def split_next(landed, done, slot):
                act.wait_ge(unit_done, done)
                act.wait_ge(raw_loaded[slot], landed)
                nc.scalar.activation(whi[slot][:], raw[slot][:], ACT.Copy).then_inc(whi_ready, 1)

            act.sem_inc(yrs_ready, 1)
            with act.Fori(0, GROUPS) as g:
                def arrive(j):
                    split_next(g * 48 + (SSM_LANDED + 16 * (j // 2 + 1)), g * 6 + (U_SSM + j + 1), j % 2)

                def tile_of(j):
                    return g * 2 + j if j < 2 else g + (16 if j == 2 else 24)

                def conv_first(j):
                    nc.scalar.activation(grp[:, j, :], bank[j % 2][:], ACT.Identity,
                                         scale=vt[:, bass.ds(tile_of(j) + (V_CW + 3 * 32), 1)],
                                         bias=vt[:, bass.ds(tile_of(j) + V_CB, 1)]).then_inc(conv_begun, 1)

                def conv_silu(j):
                    act.wait_ge(conv_summed, g * 4 + (j + 1))
                    nc.scalar.activation(grp[:, j, :], grp[:, j, :], ACT.Silu).then_inc(conv_ready, 1)

                def seg_exp(c):
                    act.wait_ge(seg_summed, g * 4 + (c + 1))
                    nc.scalar.activation(mdec[:, c].rearrange("p h l -> p (h l)"), bank[6 + c % 2][:],
                                         ACT.Exp).then_inc(dec_exp, 1)

                arrive(0)
                conv_first(0)
                seg_exp(0)
                seg_exp(1)
                arrive(1)
                conv_first(1)
                seg_exp(2)
                seg_exp(3)
                conv_silu(0)
                conv_silu(1)
                arrive(2)
                conv_first(2)
                arrive(3)
                conv_first(3)
                conv_silu(2)
                conv_silu(3)
                arrive(4)
                nc.scalar.activation(grp[:, 4, :], bank[0][:], ACT.Silu).then_inc(unit_read[0], 1)
                act.wait_ge(b_turned, g + 1)
                nc.scalar.activation(btok[:].rearrange("p c n -> p (c n)"), bank[4][:], ACT.Copy).then_inc(btok_ready, 1)
                arrive(5)
                nc.scalar.activation(grp[:, 5, :], bank[1][:], ACT.Silu).then_inc(unit_read[1], 1)
                for j in range(2):
                    act.wait_ge(eo_summed, g * 2 + (j + 1))
                    nc.scalar.activation(eo[:, j, :], bank[6 + j][:, P:S], ACT.Exp).then_inc(eo_ready, 1)
                for j in range(2):
                    act.wait_ge(y_gated, g * 2 + (j + 1))
                    nc.scalar.activation(sq[:, j, :], yt[:, j, :], ACT.Square).then_inc(ysq_ready, 1)
                act.wait_ge(yms_done, g + 1)
                nc.scalar.activation(rs, bank[6][:], ACT.Ln, bias=eps_col[:, 0:1]).then_inc(yln_ready, 1)
                act.wait_ge(yln_ready, g + 1)
                nc.scalar.activation(rs, rs, ACT.Exp, scale=-0.5).then_inc(yrs_ready, 1)
                for j in range(2):
                    act.wait_ge(yn_ready, g * 2 + (j + 1))
                    nc.scalar.activation(y_hi[:, bass.ds(g * 2 + j, 1), :], yn[:, j:j + 1, :], ACT.Copy).then_inc(yhi_ready, 1)

            with act.Fori(0, 4) as m:
                for t in range(2):
                    for i in range(5):
                        j = 5 * t + i
                        split_next(m * 80 + (MIX_LANDED + 16 * (j // 2 + 1)), m * 10 + (U_MIX + j + 1), j % 2)
                        if i in (2, 4):
                            nc.scalar.activation(sig[:, i // 2 - 1, :], bank[4 * t + (1 if i == 2 else 3)][:],
                                                 ACT.Sigmoid).then_inc(mix_sig, 1)
                    act.wait_ge(mix_sum, m * 2 + (t + 1))
                    nc.scalar.activation(m_hi[:, bass.ds(m * 2 + t, 1), :], mt[:, 0:1, :], ACT.Copy).then_inc(mhi_ready, 1)

            for j in range(8):
                split_next(WO_LANDED + 16 * (j // 2 + 1), U_WO + j + 1, j % 2)

            def norm_squares2(i, ready, count):
                act.wait_ge(ready, count)
                for c in range(NC):
                    if c:
                        act.wait_ge(n2_sumsq[i], c)
                    nc.scalar.activation(junk2[:], x1[:, c, :], ACT.Square,
                                         accum_out=stat2[:, i, c:c + 1]).then_inc(n2_sumsq[i], 1)
                act.wait_ge(n2_ms[i], 1)
                nc.scalar.activation(stat2[:, i, 8:12], stat2[:, i, 4:8], ACT.Sqrt).then_inc(n2_rms[i], 1)

            norm_squares2(0, x1_ready, 2 * NC)
            for k in range(KT):
                act.wait_ge(xn2_turned, k + 1)
                nc.scalar.activation(h_hi[:, k, :], bank[k % 4][:], ACT.Copy,
                                     scale=vt[:, V_GMLP + k:V_GMLP + k + 1]).then_inc(h2hi_ready, 1)

            def quarter(q, last):
                def split_mlp(j):
                    split_next(q * 128 + (MLP_LANDED + 16 * (j // 2 + 1)), q * 16 + (U_MLP + j + 1), j % 2)

                for j in range(9):
                    if j < 8:
                        split_mlp(j)
                        nc.scalar.activation(rel[:, j % 2, :], bank[2 + j % 2][:], ACT.Relu).then_inc(relu_ready, 1)
                    if j:
                        act.wait_ge(uf_ready, q * 8 + j)
                        nc.scalar.activation(u_hi[:, j - 1, :], uf[:, (j - 1) % 2, :], ACT.Copy).then_inc(uhi_ready, 1)
                for j in range(8, 14 if last else 16):
                    split_mlp(j)

            with act.Fori(0, 3) as q:
                quarter(q, last=False)
            quarter(3, last=True)
            norm_squares2(1, down_added, 4 + 4 * 2 * NC)


        @block.vector
        def _(dve):
            step = Steps(dve, dve_steps)
            V = nc.vector

            dve.wait_ge(const_loaded, 16)
            V.tensor_copy(ident_bf[:], ident).then_inc(masks_ready, 1)
            V.tensor_copy(causal_bf[:], cst[:, K_CB:K_CB + P]).then_inc(masks_ready, 1)

            def norm_rstd(src, dst, gate_sem):
                dve.wait_ge(gate_sem, NC)
                V.tensor_scalar(stat[:, 4:8], stat[:, 0:4], 1.0 / D, EPS, ALU.mult, ALU.add).then_inc(ms_ready, 1)

            norm_rstd(x_sb, xn, sumsq_ready)
            dve.wait_ge(rms_ready, 1)
            V.reciprocal(stat[:, 12:16], stat[:, 8:12]).then_inc(rstd_ready, 1)
            dve.wait_ge(rstd_ready, 1)
            for c in range(NC):
                V.tensor_scalar(xn[:, c, :], x_sb[:, c, :], stat[:, 12 + c:13 + c], None,
                                ALU.mult).then_inc(xn_ready, 1)
            dve.wait_ge(vec_turned, 1)
            V.tensor_copy(vt[:], bank[2][:, 0:240]).then_inc(vec_ready, 1)
            dve.wait_ge(vec_ready, 1)
            for k in range(KT):
                dve.wait_ge(hhi_ready, k + 1)
                V.scalar_tensor_tensor(h_lo[:, k, :], bank[3 + k % 4][:], vt[:, V_GMIX + k:V_GMIX + k + 1],
                                       h_hi[:, k, :].bitcast(F32), ALU.mult, ALU.subtract).then_inc(hlo_ready, 1)

            dve.wait_ge(small_loaded, 64)
            step(V.tensor_copy(rt[:, 0, :], pos_i[:]))
            step.wait()
            step(V.tensor_scalar(rt[:, 1, :], rt[:, 0, :], cst[:, K_F:K_F + 1], None, ALU.mult))
            step.wait()
            step(V.tensor_scalar(rt[:, 2, :], rt[:, 1, :], 1.0 / TWO_PI, None, ALU.mult))
            step.wait()
            step(V.tensor_scalar(rt[:, 0, :], rt[:, 2, :], MAGIC, None, ALU.add))
            step.wait()
            step(V.tensor_scalar(rt[:, 2, :], rt[:, 0, :], MAGIC, None, ALU.subtract))
            for n, part in enumerate((PI_A, PI_B, PI_C)):
                step.wait()
                step(V.scalar_tensor_tensor(rt[:, n % 2, :], rt[:, 2, :], -part, rt[:, 1 - n % 2, :],
                                            ALU.mult, ALU.add))
            step.wait()
            step(V.tensor_scalar(rt[:, 1, :], rt[:, 0, :], np.pi / 2, None, ALU.add))
            step(V.tensor_scalar(rt[:, 2, :], rt[:, 0, :], np.pi / 2, None, ALU.is_gt))
            step.wait()
            V.tensor_scalar(rt[:, 0, :], rt[:, 0, :], -SIN_MAX, SIN_MAX, ALU.max, ALU.min).then_inc(angle_ready, 1)
            step(V.scalar_tensor_tensor(rt[:, 1, :], rt[:, 2, :], -TWO_PI, rt[:, 1, :], ALU.mult, ALU.add))
            step.wait()
            V.tensor_scalar(rt[:, 1, :], rt[:, 1, :], -SIN_MAX, SIN_MAX, ALU.max, ALU.min).then_inc(angle_ready, 1)
            dve.wait_ge(sin_ready, 2)
            V.tensor_scalar(ropeS[:], ropeS[:], cst[:, K_F + 1:K_F + 2], None, ALU.mult).then_inc(rope_ready, 1)

            dve.wait_ge(unit_done, 1)
            V.tensor_scalar(dtw[:, 0, :], bank[0][0:HEADS, :], small[:, 0:1], None, ALU.add).then_inc(unit_read[0], 1)
            dve.wait_ge(unit_read[0], 1)
            V.scalar_tensor_tensor(dtw[:, 1, :], dtw[:, 0, :], -1.0, dtw[:, 0, :],
                                   ALU.mult, ALU.min).then_inc(dt_neg, 1)
            dve.wait_ge(dt_exp, 2)
            V.tensor_scalar(dtw[:, 3, :], dtw[:, 2, :], 1.0, None, ALU.add).then_inc(dt_one, 1)
            dve.wait_ge(dt_one, 1)
            step(V.tensor_scalar(dtw[:, 5, :], dtw[:, 3, :], 1.0, None, ALU.subtract))
            step.wait()
            step(V.tensor_scalar(dtw[:, 6, :], dtw[:, 5, :], 0.0, None, ALU.is_equal))
            step.wait()
            step(V.tensor_tensor(dtw[:, 5, :], dtw[:, 5, :], dtw[:, 6, :], ALU.add))
            dve.wait_ge(dt_log, 1)
            step(V.tensor_tensor(dtw[:, 7, :], dtw[:, 4, :], dtw[:, 6, :], ALU.add))
            step.wait()
            step(V.reciprocal(dtw[:, 3, :], dtw[:, 5, :]))
            step.wait()
            step(V.tensor_tensor(dtw[:, 7, :], dtw[:, 7, :], dtw[:, 3, :], ALU.mult))
            step.wait()
            step(V.tensor_tensor(dtw[:, 7, :], dtw[:, 7, :], dtw[:, 2, :], ALU.mult))
            step.wait()
            V.scalar_tensor_tensor(dtw[:, 1, :], dtw[:, 0, :], 0.0, dtw[:, 7, :], ALU.max, ALU.add).then_inc(dt_ready, 1)
            dve.wait_ge(dt_ready, 1)
            V.tensor_scalar(dtw[:, 4, :], dtw[:, 1, :], small[:, 2:3], -1.0, ALU.mult, ALU.mult).then_inc(dt_ready, 1)

            for j in range(12):
                u = U_KV + j
                kind, pp = divmod(j, 2)
                if kind < 2:
                    dve.wait_ge(unit_done, u + 1)
                    for e in range(2):
                        src = bank[u % 2][e * HD:(e + 1) * HD, :]
                        step(V.tensor_copy(kcx[0:HD, kind, 2 * pp + e, :], src))
                        ins = V.tensor_copy(kcx[HD:P, kind, 2 * pp + e, 0:S - 1], src[:, 1:S])
                        if e == 0:
                            step(ins)
                        else:
                            ins.then_inc(unit_read[u % 2], 1)
                elif kind in (2, 4):
                    b = kind // 4
                    dve.wait_ge(unit_done, u + 1)
                    V.tensor_copy(kT[:, b, pp, :], bank[u % 2][:]).then_inc(unit_read[u % 2], 1)
                    dve.wait_ge(k_swapped, 2 * b + pp + 1)
                    dve.wait_ge(rope_ready, 1)
                    if b or pp:
                        dve.wait_ge(k_ready, 2 * b + pp)
                    step(V.tensor_tensor(rtmp[:], bank[6 + pp][:], ropeS[:], ALU.mult))
                    step(V.tensor_tensor(kT[:, b, pp, :], kT[:, b, pp, :], ropeC[:], ALU.mult))
                    step.wait()
                    V.tensor_tensor(kT[:, b, pp, :], kT[:, b, pp, :], rtmp[:], ALU.add).then_inc(k_ready, 1)
                if j == 1:
                    dve.wait_ge(dt_turned, 1)
                    V.tensor_copy(dtT[:].rearrange("p a c h -> p (a c h)"), bank[2][:, 0:256]).then_inc(dtT_ready, 1)
                if j == 2:
                    dve.wait_ge(ag_turned, 1)
                    V.tensor_copy(gate[:].rearrange("p c n -> p (c n)"), bank[4][:, 0:192]).then_inc(gate_ready, 1)
                if j == 4:
                    dve.wait_ge(dec_ready, 1)
                    step(V.tensor_tensor(dd[:], dtT[:, 0], decs[:, 0], ALU.mult))

            dve.wait_ge(xn_turned, KT)
            V.memset(hid[:], 0.0).then_inc(hid_zeroed, 1)
            step(V.tensor_scalar(cbias[:], cmask, -1.0, -NEG, ALU.add, ALU.mult))
            step.wait()
            for i in range(2):
                if i:
                    dve.wait_ge(hid_summed, 1)
                for jj in range(16):
                    ins = V.tensor_scalar(blk[:, jj, 0:KVG * CMP].rearrange("p (g k) -> p g k", g=KVG),
                                          kcx[:, i, :, 2 * jj:2 * jj + 16 * (CMP - 1) + 1:16],
                                          vt[:, V_PE + 16 * i + jj:V_PE + 16 * i + jj + 1], None, ALU.add)
                    ins.then_inc(blk_ready, 1)
            dve.wait_ge(hid_ready, 2)
            hv = hid[:, 1].rearrange("p h g k -> p (h g) k")
            V.tensor_copy(hidr[:].rearrange("p h g e k -> p (h g) e k"),
                          hv.unsqueeze(2).to_broadcast([P, 8, 4, 32])).then_inc(hidr_ready, 1)
            dve.wait_ge(kvc_summed, 1)
            V.tensor_copy(kc[:].rearrange("p g k -> p (g k)"), bank[4][:, 0:P]).then_inc(kvc_ready, 1)
            dve.wait_ge(kvc_summed, 2)
            V.tensor_copy(vc[:].rearrange("p g d -> p (g d)"), bank[5][:, 0:256]).then_inc(kvc_ready, 1)

            with dve.Fori(0, 2) as rr:
                step.loop(rr, 4 * 2 + 4 * 5 + 64)
                for j in range(4):
                    dve.wait_ge(q_swapped, rr * 4 + (j + 1))
                    if j:
                        dve.wait_ge(q_ready, rr * 4 + j)
                    step(V.tensor_tensor(rtmp[:], bank[6 + j % 2][:], ropeS[:], ALU.mult))
                    step(V.tensor_tensor(q_r[:, j, :], q_s[:, j, :], ropeC[:], ALU.mult))
                    step.wait()
                    V.tensor_tensor(q_r[:, j, :], q_r[:, j, :], rtmp[:], ALU.add).then_inc(q_ready, 1)

                def cmp_read():
                    for e in range(2):
                        dve.wait_ge(cs_ready, rr * 2 + (e + 1))
                        V.tensor_tensor(cs[:, e], bank[e][:].rearrange("p (i h k) -> p i h k", i=NC, k=32),
                                        cbias[:].unsqueeze(2).to_broadcast([P, NC, 4, 32]),
                                        ALU.add).then_inc(cs_read, 1)

                def cmp_centre(i):
                    dve.wait_ge(cs_read, rr * 2 + 2)
                    if i:
                        dve.wait_ge(cp_turned, rr * NC + i)
                    step(V.tensor_reduce(cst8[:, 3, :].rearrange("p (e h) -> p e h", e=2), cs[:, :, i], AX.X, ALU.max))
                    step.wait()
                    V.tensor_tensor(cp[:, 0].rearrange("p (e h) k -> p e h k", e=2), cs[:, :, i],
                                    cst8[:, 3, :].rearrange("p (e h) -> p e h", e=2).unsqueeze(3).to_broadcast([P, 2, 4, 32]),
                                    ALU.subtract).then_inc(cs_centred, 1)

                def cmp_probs(i):
                    dve.wait_ge(cs_exp, rr * NC + (i + 1))
                    step(V.tensor_reduce(cst8[:, 0, :], cp[:, 1], AX.X, ALU.add))
                    step(V.tensor_tensor(cp[:, 0], cp[:, 1], cmask[:, i, :].unsqueeze(1).to_broadcast([P, 8, 32]),
                                         ALU.mult))
                    step.wait()
                    step(V.reciprocal(cst8[:, 1, :], cst8[:, 0, :]))
                    step.wait()
                    gates = gate[:, i, 0:16].rearrange("p (m e r) -> p e m r", m=2, e=2)[:, :, :, bass.ds(rr * 2, 2)]
                    step(V.tensor_tensor(cst8[:, 2, :].rearrange("p (e m r) -> p e m r", e=2, m=2),
                                         cst8[:, 1, :].rearrange("p (e m r) -> p e m r", e=2, m=2), gates, ALU.mult))
                    step.wait()
                    V.tensor_tensor(cp[:, 2], cp[:, 0], cst8[:, 2, :].unsqueeze(2).to_broadcast([P, 8, 32]),
                                    ALU.mult).then_inc(cp_ready, 1)

                def row_max(n):
                    dve.wait_ge(s_ready, rr * 64 + (n + 1))
                    w = (n // 16 + 1) * P
                    V.tensor_reduce(nmax[:, n % 4:n % 4 + 1], bank[1 + n % 3][:, 0:w], AX.X, ALU.max,
                                    negate=True).then_inc(max_ready, 1)

                def scale_probs(n):
                    i, b = divmod(n, 16)
                    g, r2, br = b // 4, b // 2 % 2, b % 2
                    w = (i + 1) * P
                    dve.wait_ge(exp_ready, rr * 64 + (n + 1))
                    step(V.reciprocal(rsum[:, n % 4:n % 4 + 1], esum[:, n % 4:n % 4 + 1]))
                    step.wait()
                    V.tensor_scalar(prob[n % 3][:, 0:w], prob[n % 3][:, 0:w], rsum[:, n % 4:n % 4 + 1],
                                    gate[:, i, bass.ds(rr * 2 + (16 * (br + 1) + g * R + r2), 1)],
                                    ALU.mult, ALU.mult).then_inc(prob_ready, 1)

                def low_out(g4):
                    i, g = divmod(g4, KVG)
                    dve.wait_ge(ohi_ready, rr * 16 + (g4 + 1))
                    where = (slice(None), bass.ds(rr + 2 * g, 1), slice(i * P, (i + 1) * P))
                    V.tensor_tensor(o_lo[where], bank[6 + g % 2][:, 0:P].unsqueeze(1), o_hi[where].bitcast(F32),
                                    ALU.subtract).then_inc(olo_ready, 1)

                cmp_read()
                cmp_centre(0)
                row_max(0)
                row_max(1)
                cmp_probs(0)
                for n in range(64):
                    scale_probs(n)
                    if n + 2 < 64:
                        row_max(n + 2)
                    if n < 48 and n % 16 == 5:
                        cmp_centre(n // 16 + 1)
                    if n < 48 and n % 16 == 8:
                        cmp_probs(n // 16 + 1)
                    if n % 4 == 2 and n > 4:
                        low_out(n // 4 - 1)
                low_out(15)
                step.end(2)

            steps = Steps(dve, ssm_steps)
            with dve.Fori(0, GROUPS) as g:
                steps.loop(g, 8)
                heads = bass.ds(g * HPG, HPG)

                V.tensor_copy(dtab[:].rearrange("p c (h d) -> p c h d", h=HPG),
                              dtT[:, 1, 1:NC, heads].unsqueeze(3).to_broadcast([P, NC - 1, HPG, HD])).then_inc(dtab_ready, 1)

                def seg_operand(c):
                    if c >= 2:
                        dve.wait_ge(seg_summed, g * 4 + (c - 1))
                    V.tensor_tensor(segr[:, c % 2], tri.unsqueeze(1).to_broadcast([P, HPG, P]),
                                    dtT[:, 1, c, heads].unsqueeze(2).to_broadcast([P, HPG, P]),
                                    ALU.mult).then_inc(segr_ready, 1)

                def conv(j):
                    tile = g * 2 + j if j < 2 else g + (16 if j == 2 else 24)
                    dve.wait_ge(conv_begun, g * 4 + (j + 1))
                    for back in range(1, CONV):
                        ins = V.scalar_tensor_tensor(
                            grp[:, j, back:S], bank[j % 2][:, 0:S - back],
                            vt[:, bass.ds(tile + (V_CW + (CONV - 1 - back) * 32), 1)],
                            grp[:, j, back:S], ALU.mult, ALU.add)
                        if back < CONV - 1:
                            ins.then_inc(conv_step, 1)
                            dve.wait_ge(conv_step, g * 8 + (j * 2 + back))
                        else:
                            ins.then_inc(conv_summed, 1)

                seg_operand(0)
                seg_operand(1)
                conv(0)
                seg_operand(2)
                seg_operand(3)
                conv(1)
                conv(2)
                conv(3)
                for n in range(2):
                    dve.wait_ge(x_turned, g * 2 + (n + 1))
                    src = bank[2 + n][:].rearrange("p (c h d) -> p c h d", c=2, h=HPG)
                    V.tensor_tensor(xdt[:, 2 * n:2 * n + 2].rearrange("p c (h d) -> p c h d", h=HPG), src,
                                    dtT[:, 0, 2 * n:2 * n + 2, heads].unsqueeze(3).to_broadcast([P, 2, HPG, HD]),
                                    ALU.mult).then_inc(xdt_ready, 1)
                    w = 2 - n
                    V.tensor_tensor(xdd[:, 2 * n:2 * n + w].rearrange("p c (h d) -> p c h d", h=HPG), src[:, 0:w],
                                    dd[:, 2 * n:2 * n + w, heads].unsqueeze(3).to_broadcast([P, w, HPG, HD]),
                                    ALU.mult).then_inc(xdd_ready, 1)
                dve.wait_ge(cb_done, g + 1)
                V.tensor_tensor(cbm[:], bank[5][:].rearrange("p (c l) -> p c l", c=NC),
                                tri.unsqueeze(1).to_broadcast([P, NC, P]), ALU.mult).then_inc(cbm_ready, 1)
                dve.wait_ge(cbm_ready, g + 1)
                for c in range(NC):
                    dve.wait_ge(dec_exp, g * 4 + (c + 1))
                    V.tensor_tensor(mdec[:, c], mdec[:, c], cbm[:, c, :].unsqueeze(1).to_broadcast([P, HPG, P]),
                                    ALU.mult).then_inc(mdec_ready, 1)
                dve.wait_ge(st_done, g + 1)
                V.tensor_copy(prev[:, 0, :], bank[4][:, 0:256]).then_inc(prev_ready, 1)
                for c in range(1, NC - 1):
                    dve.wait_ge(prev_ready, g * 3 + c)
                    steps(V.tensor_tensor(prev[:, c, :].rearrange("p (h d) -> p h d", h=HPG),
                                          prev[:, c - 1, :].rearrange("p (h d) -> p h d", h=HPG),
                                          decs[:, 1, c, heads].unsqueeze(2).to_broadcast([P, HPG, HD]), ALU.mult))
                    steps.wait()
                    V.tensor_tensor(prev[:, c, :], prev[:, c, :], bank[4 + c // 2][:, (c % 2) * 256:(c % 2) * 256 + 256],
                                    ALU.add).then_inc(prev_ready, 1)
                for j in range(2):
                    dve.wait_ge(yd_done, g * 2 + (j + 1))
                    steps(V.scalar_tensor_tensor(yt[:, j, :], grp[:, j, :], vt[:, bass.ds(g * 2 + (V_D + j), 1)],
                                                 bank[2 + j][:], ALU.mult, ALU.add))
                for j in range(2):
                    dve.wait_ge(eo_ready, g * 2 + (j + 1))
                    dve.wait_ge(yo_done, g * 2 + (j + 1))
                    steps(V.tensor_tensor(eo[:, j, :], bank[4 + j][:, P:S], eo[:, j, :], ALU.mult))
                    steps.wait()
                    steps(V.tensor_tensor(yt[:, j, P:S], yt[:, j, P:S], eo[:, j, :], ALU.add))
                    dve.wait_ge(unit_read[j], g + Z_READ)
                    steps.wait()
                    V.tensor_tensor(yt[:, j, :], yt[:, j, :], grp[:, 4 + j, :], ALU.mult).then_inc(y_gated, 1)
                dve.wait_ge(y_gated, g * 2 + 2)
                dve.wait_ge(yrs_ready, g + 2)
                for j in range(2):
                    V.scalar_tensor_tensor(yn[:, j, :], yt[:, j, :], vt[:, bass.ds(g * 2 + (V_GSSM + j), 1)], rs,
                                           ALU.mult, ALU.mult).then_inc(yn_ready, 1)
                for j in range(2):
                    where = bass.ds(g * 2 + j, 1)
                    dve.wait_ge(yhi_ready, g * 2 + (j + 1))
                    dve.wait_ge(yn_ready, g * 2 + (j + 1))
                    V.tensor_tensor(y_lo[:, where, :], yn[:, j:j + 1, :], y_hi[:, where, :].bitcast(F32),
                                    ALU.subtract).then_inc(ylo_ready, 1)
                steps.end(GROUPS)

            dve.sem_inc(mlo_ready, 2)
            with dve.Fori(0, 4) as m:
                for t in range(2):
                    for i in range(2):
                        dve.wait_ge(mix_sig, m * 4 + (2 * t + i + 1))
                        if i == 0:
                            dve.wait_ge(mlo_ready, m * 2 + (t + 2))
                        V.tensor_tensor(mt[:, i, :], bank[4 * t + 2 * i][:], sig[:, i, :], ALU.mult).then_inc(mix_part, 1)
                    dve.wait_ge(mix_part, m * 4 + (2 * t + 2))
                    V.tensor_tensor(mt[:, 0, :], mt[:, 0, :], mt[:, 1, :], ALU.add).then_inc(mix_sum, 1)
                    where = bass.ds(m * 2 + t, 1)
                    dve.wait_ge(mhi_ready, m * 2 + (t + 1))
                    V.tensor_tensor(m_lo[:, where, :], mt[:, 0:1, :], m_hi[:, where, :].bitcast(F32),
                                    ALU.subtract).then_inc(mlo_ready, 1)

            dve.wait_ge(x1_loaded, 16)
            for half in range(2):
                dve.wait_ge(unit_done, U_WO + 4 * half + 4)
                for c in range(NC):
                    cols = slice(half * 512, half * 512 + 512)
                    V.tensor_tensor(x1[:, c, cols], bank[4 * half + c][:], x1[:, c, cols], ALU.add).then_inc(x1_ready, 1)

            def norm_rstd2(i):
                dve.wait_ge(n2_sumsq[i], NC)
                V.tensor_scalar(stat2[:, i, 4:8], stat2[:, i, 0:4], 1.0 / D, EPS, ALU.mult, ALU.add).then_inc(n2_ms[i], 1)
                dve.wait_ge(n2_rms[i], 1)
                V.reciprocal(stat2[:, i, 12:16], stat2[:, i, 8:12]).then_inc(n2_rstd[i], 1)
                dve.wait_ge(n2_rstd[i], 1)

            norm_rstd2(0)
            for c in range(NC):
                V.tensor_scalar(xn2[:, c, :], x1[:, c, :], stat2[:, 0, 12 + c:13 + c], None, ALU.mult).then_inc(xn2_ready, 1)
            for k in range(KT):
                dve.wait_ge(h2hi_ready, k + 1)
                V.scalar_tensor_tensor(h_lo[:, k, :], bank[k % 4][:], vt[:, V_GMLP + k:V_GMLP + k + 1],
                                       h_hi[:, k, :].bitcast(F32), ALU.mult, ALU.subtract).then_inc(h2lo_ready, 1)

            dve.sem_inc(down_added, 4)
            with dve.Fori(0, 4) as q:
                for j in range(9):
                    if j < 8:
                        dve.wait_ge(relu_ready, q * 8 + (j + 1))
                        if j >= 2:
                            dve.wait_ge(ulo_ready, q * 8 + (j - 1))
                        V.tensor_tensor(uf[:, j % 2, :], rel[:, j % 2, :], rel[:, j % 2, :], ALU.mult).then_inc(uf_ready, 1)
                    if j:
                        dve.wait_ge(uhi_ready, q * 8 + j)
                        V.tensor_tensor(u_lo[:, j - 1, :], uf[:, (j - 1) % 2, :], u_hi[:, j - 1, :].bitcast(F32),
                                        ALU.subtract).then_inc(ulo_ready, 1)
                for half in range(2):
                    cols = slice(half * 512, half * 512 + 512)
                    for c in (2, 3, 0, 1):
                        dve.wait_ge(unit_done, q * 16 + (U_MLP + 8 + 4 * half + 4))
                        V.tensor_tensor(x1[:, c, cols], bank[4 * (1 - half) + c][:], x1[:, c, cols],
                                        ALU.add).then_inc(down_added, 1)

            norm_rstd2(1)
            dve.wait_ge(gfin_loaded, 16)
            for c in range(NC):
                V.scalar_tensor_tensor(xn2[:, c, :], x1[:, c, :], stat2[:, 1, 12 + c:13 + c], gfin[:],
                                       ALU.mult, ALU.mult).then_inc(out_ready, 1)

        @block.tensor
        def _(pe):
            T = nc.tensor

            def unit(u, slot, read=None):
                pe.wait_ge(whi_ready, u + 1)
                if read is not None:
                    pe.wait_ge(unit_read[slot], read)
                for k in range(KT):
                    for n, part in enumerate((h_hi, h_lo)):
                        T.matmul(bank[slot][:], whi[slot][:, k * P:(k + 1) * P], part[:, k, :],
                                 start=(k == 0 and n == 0), stop=False)
                pe.wait_ge(wlo_ready, u + 1)
                for k in range(KT):
                    mm = T.matmul(bank[slot][:], wlo[slot][:, k * P:(k + 1) * P], h_hi[:, k, :],
                                  start=False, stop=(k == KT - 1))
                mm.then_inc(unit_done, 1)

            pe.wait_ge(const_loaded, 16)
            pe.wait_ge(rows_loaded, 16 * 7)
            pe.wait_ge(small_loaded, 64)
            T.transpose(bank[2][:, 0:P], rows1[:], ident)
            T.transpose(bank[2][:, P:P + 96], rows2[:], ident[0:96, 0:96])
            T.matmul(bank[2][:, 224:240], cst[0:2, K_HALF:K_HALF + P], d_two[:],
                     start=True, stop=True).then_inc(vec_turned, 1)
            for k in range(KT):
                if k == 0:
                    pe.wait_ge(xn_ready, NC)
                if k >= 4:
                    pe.wait_ge(hlo_ready, k - 3)
                for c in range(NC):
                    mm = T.transpose(bank[3 + k % 4][:, c * P:(c + 1) * P], xn[:, c, k * P:(k + 1) * P], ident)
                mm.then_inc(xn_turned, 1)
            pe.wait_ge(hlo_ready, KT)
            unit(0, 0)
            unit(1, 1)

            def swap(src, bank_to, signal):
                T.matmul(bank_to[:], perm, src, start=True, stop=True).then_inc(signal, 1)

            def turn_v(b, pp):
                pe.wait_ge(unit_read[(U_KV + 4 * b + 6 + pp) % 2], (U_KV + 4 * b + 6 + pp) // 2 + 1)
                if b:
                    pe.wait_ge(v_ready, pp + 1)
                elif pp == 0:
                    pe.wait_ge(gate_ready, 1)
                for c in range(NC):
                    mm = T.transpose(bank[4 + pp][:, c * P:(c + 1) * P], vtmp[:, pp, c * P:(c + 1) * P], ident)
                mm.then_inc(v_turned, 1)

            def swap_k(b, pp):
                pe.wait_ge(unit_read[(U_KV + 4 * b + 4 + pp) % 2], (U_KV + 4 * b + 4 + pp) // 2 + 1)
                if b:
                    pe.wait_ge(k_ready, pp + 1)
                swap(kT[:, b, pp, :], bank[6 + pp], k_swapped)

            for j in range(12):
                u = U_KV + j
                unit(u, u % 2, u // 2)
                if j == 1:
                    pe.wait_ge(dt_ready, 2)
                    pe.wait_ge(vec_ready, 1)
                    for i, row in enumerate((1, 4)):
                        for c in range(NC):
                            n = (i * NC + c) * HEADS
                            mm = T.transpose(bank[2][:, n:n + HEADS], dtw[:, row, c * P:(c + 1) * P],
                                             ident[0:HEADS, 0:HEADS])
                    mm.then_inc(dt_turned, 1)
                if j == 2:
                    pe.wait_ge(unit_read[1], 1)
                    for c in range(NC):
                        mm = T.transpose(bank[4][:, c * 48:(c + 1) * 48], ag[:, c * P:(c + 1) * P],
                                         ident[0:48, 0:48])
                    mm.then_inc(ag_turned, 1)
                    pe.wait_ge(dtT_ready, 1)
                    pe.wait_ge(ones_set, 3)
                    dta = dtT[:, 1].rearrange("p c h -> p (c h)")
                    T.matmul(bank[3][:, 0:P], stri, dta, start=True, stop=True)
                    T.matmul(bank[3][:, P:2 * P], ones[:], dta, start=True, stop=True).then_inc(dec_summed, 1)
                if j in (5, 6, 9, 10):
                    swap_k(j // 8, (j - 1) % 2)
                if j in (7, 8, 11):
                    turn_v(j // 10, (j - 1) % 2)
            turn_v(1, 1)

            pe.wait_ge(cmpw_loaded, 16 * 6)
            for i in range(2):
                if i == 0:
                    pe.wait_ge(dec_ready, 1)
                for half in range(2):
                    for jj in range(16):
                        if half == 0:
                            pe.wait_ge(blk_ready, 16 * i + jj + 1)
                        mm = T.matmul(bank[2 + i][:, half * P:(half + 1) * P].rearrange("p (g k) -> p g k", k=32)[:, :, 0:CMP],
                                      w1c[:, i, jj, half * P:(half + 1) * P],
                                      blk[:, jj, 0:KVG * CMP].rearrange("p (g k) -> p g k", k=CMP),
                                      start=(jj == 0), stop=(jj == 15))
                mm.then_inc(hid_summed, 1)
            pe.wait_ge(hid_ready, 1)
            pe.wait_ge(v_ready, 4)
            for half in range(2):
                mm = T.matmul(bank[4][:, 0:P], w2c[:, 0, half].rearrange("p e d -> p (e d)"),
                              hid[:, 0, half].rearrange("p g k -> p (g k)"), start=(half == 0), stop=(half == 1))
            mm.then_inc(kvc_summed, 1)
            pe.wait_ge(hidr_ready, 1)
            for g in range(KVG):
                for half in range(2):
                    mm = T.matmul(bank[5][:, g * HD:(g + 1) * HD], hidr[:, half, g].rearrange("p e k -> p (e k)"),
                                  w2c[:, 1, half, 0, :], start=(half == 0), stop=(half == 1))
            mm.then_inc(kvc_summed, 1)
            pe.wait_ge(kvc_ready, 2)
            pe.wait_ge(k_ready, 4)

            with pe.Fori(0, 2) as rr:
                for j in range(4):
                    u = rr * 4 + (U_Q + j)
                    if j < 2:
                        pe.wait_ge(unit_read[j], U_Q // 2)
                        unit(u, j % 2)
                    else:
                        pe.wait_ge(q_copied, rr * 4 + (j - 1))
                        unit(u, j % 2)
                    if j:
                        if j == 3:
                            pe.wait_ge(q_ready, rr * 4 + 1)
                        pe.wait_ge(q_copied, rr * 4 + j)
                        swap(q_s[:, j - 1, :], bank[6 + (j - 1) % 2], q_swapped)
                pe.wait_ge(q_ready, rr * 4 + 2)
                pe.wait_ge(q_copied, rr * 4 + 4)
                swap(q_s[:, 3, :], bank[7], q_swapped)

                def cmp_scores():
                    for e in range(2):
                        rows = slice(e * HD, (e + 1) * HD)
                        for i in range(NC):
                            for m in range(4):
                                n = (i * 4 + m) * 32
                                mm = T.matmul(bank[e][:, n:n + 32], q_s[rows, m, i * P:(i + 1) * P],
                                              kc[rows, m // 2 * 2 + e, :], start=True, stop=True)
                        mm.then_inc(cs_ready, 1)

                def cmp_turn(i):
                    pe.wait_ge(cp_ready, rr * NC + (i + 1))
                    if i:
                        pe.wait_ge(pcT_ready, rr * NC + i)
                    for t in range(2):
                        mm = T.transpose(bank[0][:, t * P:(t + 1) * P],
                                         cp[:, 2, 4 * t:4 * t + 4, :].rearrange("p h k -> p (h k)"), ident)
                    mm.then_inc(cp_turned, 1)

                def scores(n):
                    i, b = divmod(n, 16)
                    g, r2, br = b // 4, b // 2 % 2, b % 2
                    pp, e = divmod(g, 2)
                    rows = slice(e * HD, (e + 1) * HD)
                    if n >= 3:
                        pe.wait_ge(exp_ready, rr * 64 + (n - 2))
                    to = bank[1 + n % 3]
                    T.matmul(to[:, 0:(i + 1) * P], q_r[rows, 2 * pp + r2, i * P:(i + 1) * P],
                             kT[rows, br, pp, 0:(i + 1) * P], start=True, stop=True)
                    T.matmul(to[:, i * P:(i + 1) * P], ident_bf[:], causal_bf[:],
                             start=False, stop=True, skip_group_check=True).then_inc(s_ready, 1)

                def turn(n):
                    pe.wait_ge(prob_ready, rr * 64 + (n + 1))
                    if n >= 2:
                        pe.wait_ge(pT_ready, rr * 64 + (n - 1))
                    for t in range(n // 16 + 1):
                        mm = T.transpose(bank[4 + n % 2][:, t * P:(t + 1) * P], prob[n % 3][:, t * P:(t + 1) * P], ident)
                    mm.then_inc(prob_turned, 1)

                def weigh(n):
                    i, b = divmod(n, 16)
                    g, r2, br = b // 4, b // 2 % 2, b % 2
                    to = bank[6 + g % 2][r2 * HD:(r2 + 1) * HD, 0:P]
                    if b % 4 == 0 and n >= 8:
                        pe.wait_ge(olo_ready, rr * 16 + (n // 4 - 1))
                    if br == 0:
                        pe.wait_ge(pcT_ready, rr * NC + (i + 1))
                        t, m = g % 2, g // 2 * 2 + r2
                        rows = slice(32 * m, 32 * m + 32)
                        T.matmul(to, vc[rows, g, :], pcT[i % 2][rows, t, :], start=True, stop=False)
                    pe.wait_ge(pT_ready, rr * 64 + (n + 1))
                    for t in range(i + 1):
                        mm = T.matmul(to, vtok[:, br, t, g * HD:(g + 1) * HD], pT[n % 2][:, t * P:(t + 1) * P],
                                      start=False, stop=(br == 1 and t == i))
                    mm.then_inc(pv_done, 1)

                cmp_scores()
                pe.wait_ge(q_ready, rr * 4 + 4)
                pe.wait_ge(cs_read, rr * 2 + 2)
                scores(0)
                scores(1)
                cmp_turn(0)
                for n in range(64):
                    if n + 2 < 64:
                        scores(n + 2)
                    turn(n)
                    if n:
                        weigh(n - 1)
                    if n % 16 == 11 and n < 48:
                        cmp_turn(n // 16 + 1)
                weigh(63)
                pe.wait_ge(olo_ready, rr * 16 + 16)

            with pe.Fori(0, GROUPS) as g:
                def group_unit(j):
                    if j < 2:
                        pe.wait_ge(unit_read[j], g + Z_READ - 1)
                    else:
                        pe.wait_ge(conv_summed, g * 4 + (j - 1))
                    unit(g * 6 + (U_SSM + j), j % 2)

                def seg(c):
                    pe.wait_ge(segr_ready, g * 4 + (c + 1))
                    if c >= 2:
                        pe.wait_ge(dec_exp, g * 4 + (c - 1))
                    elif c == 0:
                        pe.wait_ge(yrs_ready, g + 1)
                    T.matmul(bank[6 + c % 2][:], stri, segr[:, c % 2].rearrange("p h l -> p (h l)"),
                             start=True, stop=True).then_inc(seg_summed, 1)

                group_unit(0)
                seg(0)
                seg(1)
                group_unit(1)
                seg(2)
                seg(3)
                group_unit(2)
                group_unit(3)
                group_unit(4)
                pe.wait_ge(conv_ready, g * 4 + 2)
                for n in range(2):
                    for c in range(2 * n, 2 * n + 2):
                        for j in range(2):
                            mm = T.transpose(bank[2 + n][:, (c % 2) * 256 + j * P:(c % 2) * 256 + (j + 1) * P],
                                             grp[:, j, c * P:(c + 1) * P], ident)
                    mm.then_inc(x_turned, 1)
                pe.wait_ge(conv_ready, g * 4 + 3)
                for c in range(NC):
                    mm = T.transpose(bank[4][:, c * P:(c + 1) * P], grp[:, 2, c * P:(c + 1) * P], ident)
                mm.then_inc(b_turned, 1)
                pe.wait_ge(conv_ready, g * 4 + 4)
                for c in range(NC):
                    tok = slice(c * P, (c + 1) * P)
                    mm = T.matmul(bank[5][:, tok], grp[:, 2, tok], grp[:, 3, tok], start=True, stop=True)
                mm.then_inc(cb_done, 1)
                group_unit(5)
                pe.wait_ge(xdd_ready, g * 2 + 2)
                pe.wait_ge(btok_ready, g + 1)
                pe.wait_ge(cbm_ready, g + 1)
                for c in range(NC - 1):
                    mm = T.matmul(bank[4 + c // 2][:, (c % 2) * 256:(c % 2) * 256 + 256], btok[:, c, :], xdd[:, c, :],
                                  start=True, stop=True)
                mm.then_inc(st_done, 1)
                pe.wait_ge(mdec_ready, g * 4 + 4)
                for j in range(2):
                    for c in range(NC):
                        for e in range(2):
                            h = 2 * j + e
                            mm = T.matmul(bank[2 + j][e * HD:(e + 1) * HD, c * P:(c + 1) * P],
                                          xdt[:, c, h * HD:(h + 1) * HD], mdec[:, c, h, :], start=True, stop=True)
                    mm.then_inc(yd_done, 1)
                for j in range(2):
                    for c in range(1, NC):
                        mm = T.matmul(bank[6 + j][:, c * P:(c + 1) * P], dtab[:, c - 1, j * P:(j + 1) * P], tri,
                                      start=True, stop=True)
                    mm.then_inc(eo_summed, 1)
                pe.wait_ge(prev_ready, g * 3 + 3)
                for j in range(2):
                    for c in range(1, NC):
                        mm = T.matmul(bank[4 + j][:, c * P:(c + 1) * P], prev[:, c - 1, j * P:(j + 1) * P],
                                      grp[:, 3, c * P:(c + 1) * P], start=True, stop=True)
                    mm.then_inc(yo_done, 1)
                pe.wait_ge(eo_ready, g * 2 + 1)
                for j in range(2):
                    pe.wait_ge(ysq_ready, g * 2 + (j + 1))
                    mm = T.matmul(bank[6][:], mean_ssm[:], sq[:, j, :], start=(j == 0), stop=(j == 1))
                mm.then_inc(yms_done, 1)

            def product(u, slot, to, hi, lo, k0, start, stop):
                pe.wait_ge(whi_ready, u + 1)
                for k in range(KT):
                    for n, part in enumerate((hi, lo)):
                        T.matmul(to[:], whi[slot][:, k * P:(k + 1) * P], part[:, k0 + k, :],
                                 start=(start and k == 0 and n == 0), stop=False)
                pe.wait_ge(wlo_ready, u + 1)
                for k in range(KT):
                    mm = T.matmul(to[:], wlo[slot][:, k * P:(k + 1) * P], hi[:, k0 + k, :],
                                  start=False, stop=(stop and k == KT - 1))
                mm.then_inc(unit_done, 1)

            def product_rows(u, slot, banks, hi, lo, k0, start, stop):
                pe.wait_ge(whi_ready, u + 1)
                for c in range(NC):
                    tok = slice(c * P, (c + 1) * P)
                    for k in range(2):
                        for n, part in enumerate((hi, lo)):
                            T.matmul(banks[c][:], part[:, k0 + k, tok], whi[slot][:, k * 512:(k + 1) * 512],
                                     start=(start and k == 0 and n == 0), stop=False)
                pe.wait_ge(wlo_ready, u + 1)
                for c in range(NC):
                    tok = slice(c * P, (c + 1) * P)
                    for k in range(2):
                        mm = T.matmul(banks[c][:], hi[:, k0 + k, tok], wlo[slot][:, k * 512:(k + 1) * 512],
                                      start=False, stop=(stop and k == 1))
                return mm

            pe.wait_ge(ylo_ready, 2 * GROUPS)
            pe.wait_ge(unit_read[0], U_Q // 2 + GROUPS)
            pe.wait_ge(unit_read[1], U_Q // 2 + GROUPS)
            with pe.Fori(0, 4) as m:
                for t in range(2):
                    pe.wait_ge(mlo_ready, m * 2 + (t + 1))
                    for i, (b, hi, lo, k0, start, stop) in enumerate((
                            (0, y_hi, y_lo, 0, True, False), (0, y_hi, y_lo, KT, False, True),
                            (1, h_hi, h_lo, 0, True, True), (2, o_hi, o_lo, 0, True, True),
                            (3, h_hi, h_lo, 0, True, True))):
                        j = 5 * t + i
                        product(m * 10 + (U_MIX + j), j % 2, bank[4 * t + b], hi, lo, k0, start, stop)

            pe.wait_ge(mlo_ready, KT + 2)
            for j in range(8):
                half, kb = divmod(j, 4)
                mm = product_rows(U_WO + j, j % 2, bank[4 * half:4 * half + 4], m_hi, m_lo, 2 * kb, kb == 0, kb == 3)
                mm.then_inc(unit_done, 1)

            for k in range(KT):
                if k == 0:
                    pe.wait_ge(xn2_ready, NC)
                if k >= 4:
                    pe.wait_ge(h2lo_ready, k - 3)
                for c in range(NC):
                    mm = T.transpose(bank[k % 4][:, c * P:(c + 1) * P], xn2[:, c, k * P:(k + 1) * P], ident)
                mm.then_inc(xn2_turned, 1)
            pe.wait_ge(h2lo_ready, KT)

            with pe.Fori(0, 4) as q:
                for j in range(8):
                    if j >= 2:
                        pe.wait_ge(relu_ready, q * 8 + (j - 1))
                    else:
                        pe.wait_ge(down_added, q * 8 + (j + 1))
                    product(q * 16 + (U_MLP + j), j % 2, bank[2 + j % 2], h_hi, h_lo, 0, True, True)
                for j in range(8):
                    half, kb = divmod(j, 4)
                    if kb == 0 and half == 1:
                        pe.wait_ge(relu_ready, q * 8 + 8)
                        pe.wait_ge(down_added, q * 8 + 4)
                    pe.wait_ge(ulo_ready, q * 8 + (2 * kb + 2))
                    mm = product_rows(q * 16 + (U_MLP + 8 + j), j % 2, bank[4 * (1 - half):4 * (1 - half) + 4],
                                      u_hi, u_lo, 2 * kb, kb == 0, kb == 3)
                    mm.then_inc(unit_done, 1)

def kernel(**inputs):
    import numpy as _np
    import concourse.bacc as _bacc
    from concourse import mybir as _mybir
    from concourse.bass_utils import run_bass_kernel_spmd as _run

    nc = _bacc.Bacc("TRN2", target_bir_lowering=False, num_devices=1)
    arrays, args = {}, {}
    inputs = dict(inputs, consts=shape_constants())
    for name, value in inputs.items():
        v = _np.ascontiguousarray(value)
        arrays[f"in_{name}"] = v
        args[name] = nc.dram_tensor(f"in_{name}", v.shape, _mybir.dt.from_np(v.dtype), kind="ExternalInput").ap()
    out = nc.dram_tensor("out", (1, S, D), F32, kind="ExternalOutput").ap()
    build(nc, args, out)
    r = _run(nc, [arrays], core_ids=[0])
    return r.results[0]["out"]
```

```python
from contextlib import ExitStack

import numpy as np

import concourse.bass as bass
from concourse import mybir

F32 = mybir.dt.float32
F32R = mybir.dt.float32r
BF16 = mybir.dt.bfloat16
I32 = mybir.dt.int32
ALU = mybir.AluOpType
ACT = mybir.ActivationFunctionType
AX = mybir.AxisListType

P = 128
S = 512
D = 1024
KT = D // P
NC = S // P
D_INNER = 2048
HEADS = 32
GROUPS = 8
HPG = HEADS // GROUPS
N_STATE = 128
XBC = D_INNER + 2 * GROUPS * N_STATE
CONV = 4
HD = 64
A_HEADS = 16
KVG = 4
R = A_HEADS // KVG
CMP = (S - 32) // 16 + 1
CMP_HID = 256
HIDDEN = 4 * D
EPS = 1e-6
NEG = -1e30

C_Z = 0
C_XS = D_INNER
C_B = C_XS + D_INNER
C_C = C_B + GROUPS * N_STATE
C_DT = C_XS + XBC
C_Q = C_DT + HEADS
C_KV = C_Q + A_HEADS * HD
C_AG = C_KV + 6 * KVG * HD
C_MIX = C_AG + 3 * A_HEADS

U_SMALL = 0
U_KV = 2
U_Q = U_KV + 12
U_SSM = U_Q + 8
U_MIX = U_SSM + 6 * GROUPS
U_WO = U_MIX + 40
U_MLP = U_WO + 8
UNITS = U_MLP + 64

K_ID, K_TRI, K_STRI, K_PERM, K_CB, K_CM, K_F = 0, 128, 256, 384, 512, 640, 768
K_HALF = 770
K_N = 770 + 128

MAGIC = 12582912.0
TWO_PI = 2 * np.pi
PI_A = 6.28125
PI_B = float(np.float32(np.round((TWO_PI - PI_A) * 2**20) / 2**20))
PI_C = float(TWO_PI - PI_A - PI_B)
SIN_MAX = 3.1415925


def shape_constants():
    c = np.zeros((P, K_N), np.float32)
    i = np.arange(P)[:, None]
    j = np.arange(P)[None, :]
    c[:, K_ID:K_ID + P] = i == j
    c[:, K_TRI:K_TRI + P] = i <= j
    c[:, K_STRI:K_STRI + P] = i > j
    d = np.arange(P) % HD
    partner = np.where(d < 8, np.arange(P) + 8, np.arange(P) - 8)
    rot = d < 16
    for p in range(P):
        if rot[p]:
            c[partner[p], K_PERM + p] = 1.0
    c[:, K_CB:K_CB + P] = np.where(j <= i, 0.0, NEG)
    for t in range(NC):
        k = np.arange(32)[None, :]
        c[:, K_CM + 32 * t:K_CM + 32 * t + 32] = (16 * k + 31 <= P * t + i) & (k < CMP)
    inv = (np.float32(500000.0) ** (-np.arange(0, 16, 2, dtype=np.float32) / np.float32(16))).astype(np.float32)
    c[:, K_F] = np.where(rot, inv[d % 8], 0.0)
    c[:, K_F + 1] = np.where(rot, np.where(d < 8, -1.0, 1.0), 0.0)
    c[0, K_HALF:K_HALF + HD] = 1.0
    c[1, K_HALF + HD:K_HALF + P] = 1.0
    return c


class Steps:

    def __init__(self, eng, sem):
        self.eng, self.sem, self.n, self.base = eng, sem, 0, 0

    def __call__(self, ins):
        ins.then_inc(self.sem, 1)
        self.n += 1

    def wait(self):
        self.eng.wait_ge(self.sem, self.base + self.n)

    def loop(self, it, per):
        self.before, self.per = self.n, per
        self.base, self.n = self.before + it * per, 0

    def end(self, rounds):
        assert self.n == self.per, (self.n, self.per)
        self.base, self.n = 0, self.before + rounds * self.per


def build(nc, a, out):
    ctx = ExitStack()
    with ctx:
        sem_names = {}

        def sem(name):
            return ctx.enter_context(nc.semaphore(name))

        at = [16512]

        def sb(name, shape, dt=F32, offset=None):
            size = 4 if dt in (F32, F32R, I32) else 2
            nbytes = (int(np.prod(shape[1:])) * size + 31) // 32 * 32
            where = at[0] if offset is None else offset
            if offset is None:
                at[0] += nbytes
            assert where + nbytes <= 229344, (name, where + nbytes)
            return nc.alloc_sbuf_tensor_at(name, list(shape), dt, offset=where)

        cst = sb("cst", [P, K_N])
        ident = cst[:, K_ID:K_ID + P]
        tri = cst[:, K_TRI:K_TRI + P]
        stri = cst[:, K_STRI:K_STRI + P]
        perm = cst[:, K_PERM:K_PERM + P]
        cmask = cst[:, K_CM:K_CM + 128].rearrange("p (t k) -> p t k", t=NC)
        ones = sb("ones", [P, P])
        mean_ssm = sb("mean_ssm", [P, P])
        ident_bf = sb("ident_bf", [P, P], BF16)
        causal_bf = sb("causal_bf", [P, P], BF16)
        vt = sb("vt", [P, 240])
        eps_col = sb("eps_col", [P, 8])
        stat = sb("stat", [P, 16])
        gate = sb("gate", [P, NC, 48])
        dtT = sb("dtT", [P, 2, NC, HEADS])
        decs = sb("decs", [P, 2, NC, HEADS])
        dta_parts = sb("dta_parts", [P, 2, NC, HEADS], F32R)
        stri_r = sb("stri_r", [P, P], F32R)
        dd = sb("dd", [P, NC, HEADS])
        raw = [sb(f"raw{i}", [P, KT * P]) for i in range(2)]
        whi = [sb(f"whi{i}", [P, KT * P], F32R) for i in range(2)]
        wlo = [sb(f"wlo{i}", [P, KT * P], F32R) for i in range(2)]
        h_hi = sb("h_hi", [P, KT, S], F32R)
        h_lo = sb("h_lo", [P, KT, S], F32R)
        o_hi = sb("o_hi", [P, KT, S], F32R)
        o_lo = sb("o_lo", [P, KT, S], F32R)
        region = at[0]

        x_sb = sb("x_sb", [P, NC, D])
        xn = sb("xn", [P, NC, D])
        sq_junk = sb("sq_junk", [P, D])
        dtw = sb("dtw", [HEADS, 8, S])
        rows1 = sb("rows1", [P, P])
        rows2 = sb("rows2", [96, P])
        small = sb("small", [HEADS, 4])
        d_two = sb("d_two", [2, HEADS // 2])
        ag = sb("ag", [48, S])
        at[0] = region
        kcx_at = at[0]
        kcx = sb("kcx", [P, 2, KVG, S])
        kT_at = at[0]
        kT = sb("kT", [P, 2, 2, S])
        vtok = sb("vtok", [P, 2, NC, KVG * HD])
        assert at[0] <= region + 2 * 4 * NC * D
        at[0] = region + 2 * 4 * NC * D + 4 * D + 8 * 4 * S + 3 * 4 * S
        w1c = sb("w1c", [P, 2, 16, CMP_HID], offset=at[0] - 0)
        at[0] += 32768
        w2c = sb("w2c", [P, 2, 2, 2, HD])
        ropeC = sb("ropeC", [P, S])
        ropeS = sb("ropeS", [P, S])
        pos_i = sb("pos_i", [P, S], I32)
        rt_at = at[0]
        rt = sb("rt", [P, 3, S])
        cs = sb("cs", [P, 2, NC, 4, 32], offset=rt_at)
        vtmp = sb("vtmp", [P, 2, S])
        cmp_end = at[0]
        at[0] = region + 2 * 4 * NC * D
        kc = sb("kc", [P, 2, P])
        vc = sb("vc", [P, KVG, HD])
        cbias = sb("cbias", [P, NC, 32])
        rtmp = sb("rtmp", [P, S])
        hid_at = at[0]
        blk = sb("blk", [P, 16, P])
        hid = sb("hid", [P, 2, 2, KVG, 32])
        hidr = sb("hidr", [P, 2, KVG, 4, 32])
        assert at[0] <= region + 2 * 4 * NC * D + 4 * D + 8 * 4 * S
        at[0] = hid_at
        kk = [[sb(f"ks{part}", [P, KVG, S], F32R) for part in range(2)]]
        pcT = [sb(f"pcT{i}", [P, 2, P]) for i in range(2)]
        assert at[0] <= region + 2 * 4 * NC * D + 4 * D + 8 * 4 * S + 3 * 4 * S
        at[0] = kcx_at
        kk.append([sb(f"kw{part}", [P, KVG, S], F32R) for part in range(2)])
        assert at[0] == kT_at
        prob = [sb(f"prob{i}", [P, S]) for i in range(4)]
        at[0] = region + 2 * 4 * NC * D + 4 * D + 8 * 4 * S + 3 * 4 * S
        q_s = sb("q_s", [P, 4, S])
        q_hl = sb("q_hl", [P, 8, S], F32R)
        pT = [sb(f"pT{i}", [P, S]) for i in range(2)]
        cp = sb("cp", [P, 3, 8, 32])
        nmax = sb("nmax", [P, 4])
        esum = sb("esum", [P, 4])
        rsum = sb("rsum", [P, 4])
        cst8 = sb("cst8", [P, 4, 8])
        assert at[0] <= region + 2 * 4 * NC * D + 4 * D + 8 * 4 * S + 3 * 4 * S + 32768

        at[0] = region
        y_hi = sb("y_hi", [P, 2 * KT, S], F32R)
        y_lo = sb("y_lo", [P, 2 * KT, S], F32R)
        after_y = at[0]
        grp = sb("grp", [P, 6, S])
        xdt = sb("xdt", [P, NC, HPG * HD])
        xdd_at = at[0]
        xdd = sb("xdd", [P, NC - 1, HPG * HD])
        btok = sb("btok", [P, NC, N_STATE])
        cbm = sb("cbm", [P, NC, P])
        seg_hi = sb("seg_hi", [P, HPG, P], F32R)
        seg_lo = sb("seg_lo", [P, HPG, P], F32R)
        mdec = sb("mdec", [P, NC, HPG, P])
        prev = sb("prev", [P, NC - 1, HPG * HD])
        dtab = sb("dtab", [P, NC - 1, HPG * HD])
        yt = sb("yt", [P, 2, S])
        eo = sb("eo", [P, 2, (NC - 1) * P], offset=xdd_at)
        ssm_end = at[0]
        sq = xdt[:].rearrange("p (j c) n -> p j (c n)", j=2)
        rs = btok[:].rearrange("p c n -> p (c n)")
        at[0] = after_y
        m_hi = sb("m_hi", [P, KT, S], F32R)
        m_lo = sb("m_lo", [P, KT, S], F32R)
        sig = sb("sig", [P, 2, S])
        mt = sb("mt", [P, 2, S])
        mix_end = at[0]
        at[0] = region
        x1 = sb("x1", [P, NC, D])
        xn2 = sb("xn2", [P, NC, D])
        u_hi = sb("u_hi", [P, KT, S], F32R)
        u_lo = sb("u_lo", [P, KT, S], F32R)
        assert at[0] <= after_y
        at[0] = after_y
        rel = sb("rel", [P, 2, S])
        uf = sb("uf", [P, 2, S])
        junk2 = o_hi[:, 0:2, :]
        at[0] = mix_end
        gfin = sb("gfin", [P, D])
        stat2 = sb("stat2", [P, 2, 24])

        V_CW, V_CB, V_GMIX, V_GSSM, V_GMLP, V_PE, V_D = 0, 128, 160, 168, 184, 192, 224

        bank = [ctx.enter_context(nc.psum_tensor(f"bank{i}", [P, 512], F32)) for i in range(8)]

        raw_loaded = [sem(f"raw_loaded{i}") for i in range(2)]
        whi_ready = sem("whi_ready")
        wlo_ready = sem("wlo_ready")
        unit_done = sem("unit_done")
        unit_read = [sem(f"unit_read{i}") for i in range(2)]
        const_loaded = sem("const_loaded")
        x_loaded = [sem(f"x_loaded{i}") for i in range(NC)]
        rows_loaded = sem("rows_loaded")
        small_loaded = sem("small_loaded")
        cmpw_loaded = sem("cmpw_loaded")
        ones_set = sem("ones_set")
        vec_turned = sem("vec_turned")
        vec_ready = sem("vec_ready")
        sumsq_ready = sem("sumsq_ready")
        rms_ready = sem("rms_ready")
        rstd_ready = sem("rstd_ready")
        xn_ready = sem("xn_ready")
        xn_turned = sem("xn_turned")
        hhi_ready = sem("hhi_ready")
        hlo_ready = sem("hlo_ready")
        masks_ready = sem("masks_ready")
        dve_steps = sem("dve_steps")
        dt_neg = sem("dt_neg")
        dt_exp = sem("dt_exp")
        dt_one = sem("dt_one")
        dt_log = sem("dt_log")
        dt_ready = sem("dt_ready")
        dt_turned = sem("dt_turned")
        dtT_ready = sem("dtT_ready")
        dec_summed = sem("dec_summed")
        dec_ready = sem("dec_ready")
        ag_ready = sem("ag_ready")
        ag_turned = sem("ag_turned")
        gate_ready = sem("gate_ready")
        angle_ready = sem("angle_ready")
        sin_ready = sem("sin_ready")
        rope_ready = sem("rope_ready")
        k_copied = sem("k_copied")
        k_swapped = sem("k_swapped")
        k_ready = sem("k_ready")
        v_copied = sem("v_copied")
        v_turned = sem("v_turned")
        v_ready = sem("v_ready")
        kcx_ready = sem("kcx_ready")
        blk_ready = sem("blk_ready")
        hid_summed = sem("hid_summed")
        hid_ready = sem("hid_ready")
        hid_zeroed = sem("hid_zeroed")
        hidr_ready = sem("hidr_ready")
        kvc_summed = sem("kvc_summed")
        kvc_ready = sem("kvc_ready")
        q_copied = sem("q_copied")
        q_swapped = sem("q_swapped")
        q_cos_ready = sem("q_cos_ready")
        q_ready = sem("q_ready")
        qhi_ready = sem("qhi_ready")
        qlo_ready = sem("qlo_ready")
        kkhi_ready = sem("kkhi_ready")
        kklo_ready = sem("kklo_ready")
        cs_ready = sem("cs_ready")
        cs_read = sem("cs_read")
        cs_centred = sem("cs_centred")
        cs_exp = sem("cs_exp")
        cp_ready = sem("cp_ready")
        cp_turned = sem("cp_turned")
        pcT_ready = sem("pcT_ready")
        s_ready = sem("s_ready")
        max_ready = sem("max_ready")
        exp_ready = sem("exp_ready")
        prob_ready = sem("prob_ready")
        prob_turned = sem("prob_turned")
        pT_ready = sem("pT_ready")
        pv_done = sem("pv_done")
        ohi_ready = sem("ohi_ready")
        olo_ready = sem("olo_ready")

        segr_ready = sem("segr_ready")
        dta_split = sem("dta_split")
        seg_summed = sem("seg_summed")
        dec_exp = sem("dec_exp")
        dtab_ready = sem("dtab_ready")
        conv_begun = sem("conv_begun")
        conv_step = sem("conv_step")
        conv_summed = sem("conv_summed")
        conv_ready = sem("conv_ready")
        z_ready = sem("z_ready")
        x_turned = sem("x_turned")
        b_turned = sem("b_turned")
        btok_ready = sem("btok_ready")
        cb_done = sem("cb_done")
        cbm_ready = sem("cbm_ready")
        xdt_ready = sem("xdt_ready")
        xdd_ready = sem("xdd_ready")
        mdec_ready = sem("mdec_ready")
        st_done = sem("st_done")
        prev_ready = sem("prev_ready")
        yd_done = sem("yd_done")
        eo_summed = sem("eo_summed")
        eo_ready = sem("eo_ready")
        yo_done = sem("yo_done")
        y_gated = sem("y_gated")
        ysq_ready = sem("ysq_ready")
        yms_done = sem("yms_done")
        yln_ready = sem("yln_ready")
        yrs_ready = sem("yrs_ready")
        yn_ready = sem("yn_ready")
        yhi_ready = sem("yhi_ready")
        ylo_ready = sem("ylo_ready")
        ssm_steps = sem("ssm_steps")
        mix_sig = sem("mix_sig")
        mix_sum = sem("mix_sum")
        mix_part = sem("mix_part")
        mhi_ready = sem("mhi_ready")
        mlo_ready = sem("mlo_ready")
        x1_loaded = sem("x1_loaded")
        gfin_loaded = sem("gfin_loaded")
        x1_ready = sem("x1_ready")
        n2_sumsq = [sem(f"n2_sumsq{i}") for i in range(2)]
        n2_pre = [sem(f"n2_pre{i}") for i in range(2)]
        n2_rms = [sem(f"n2_rms{i}") for i in range(2)]
        n2_rstd = [sem(f"n2_rstd{i}") for i in range(2)]
        sum_done = sem("sum_done")
        xn2_first = sem("xn2_first")
        xn2_ready = sem("xn2_ready")
        xn2_turned = sem("xn2_turned")
        h2hi_ready = sem("h2hi_ready")
        h2lo_ready = sem("h2lo_ready")
        relu_ready = sem("relu_ready")
        uf_ready = sem("uf_ready")
        uhi_ready = sem("uhi_ready")
        ulo_ready = sem("ulo_ready")
        down_added = sem("down_added")
        xg_ready = sem("xg_ready")
        out_first = sem("out_first")
        out_ready = sem("out_ready")
        out_stored = sem("out_stored")

        w_in = a["w_in"][0]

        def columns(weight, row0, col, width=P):
            return weight[row0:row0 + D, bass.ds(col, width)].rearrange("(k p) n -> p k n", p=P)

        def h_bank(k):
            return bank[(0, 1, 3, 4, 5, 6, 7, 2)[k]]

        def h2_bank(k):
            return bank[(2, 3, 0, 1, 4, 5, 6, 7)[k]]

        def score_bank(n):
            return bank[(2, 3, 0, 1)[n % 4]]

        def cmp_turned(n):
            if n in (3, 4):
                return 0, n - 3
            if n < 48 and n % 16 in (11, 12):
                return n // 16 + 1, n % 16 - 11
            return None

        WO_ORDER = (0, 1, 2, 3)
        DOWN_ORDER = (2, 3, 0, 1)

        def wait_sum(eng, n, sums, done):
            if n < NC - 1:
                eng.wait_ge(sum_done, sums + (n + 1))
            else:
                eng.wait_ge(unit_done, done)

        block = ctx.enter_context(nc.Block())

        @block.sync
        def _(sp):
            sp.dma_start(cst[:], a["consts"]).then_inc(const_loaded, 16)
            for c in range(NC):
                sp.dma_start(x_sb[:, c, :], a["x"][0, c * P:(c + 1) * P, :]).then_inc(x_loaded[c], 16)
            sp.dma_start(rows1[:], a["conv_w"][0].rearrange("k (t p) -> (k t) p", p=P)).then_inc(rows_loaded, 16)
            at_row = 0
            for name in ("conv_b", "g_norm_mix", "g_ssm_norm", "g_norm_mlp"):
                n = a[name].shape[1] // P
                sp.dma_start(rows2[at_row:at_row + n, :],
                             a[name][0].rearrange("(t p) -> t p", p=P)).then_inc(rows_loaded, 16)
                at_row += n
            for name in ("cmp_pe_k", "cmp_pe_v"):
                sp.dma_start(rows2[at_row:at_row + 16, :],
                             a[name][0].rearrange("(j e) d -> j (e d)", e=2)).then_inc(rows_loaded, 16)
                at_row += 16
            with nc.allow_non_contiguous_dma(reason="a few small vectors"):
                sp.dma_start(small[:, 0:1], a["dt_bias"].rearrange("a h -> h a")).then_inc(small_loaded, 16)
                sp.dma_start(small[:, 1:2], a["a_log"].rearrange("a h -> h a")).then_inc(small_loaded, 16)
                sp.dma_start(d_two[:], a["d_skip"][0].rearrange("(t e) -> e t", e=2)).then_inc(small_loaded, 16)
            sp.dma_start(pos_i[:], a["positions"].to_broadcast([P, S])).then_inc(small_loaded, 16)

            def load(u, slot, source):
                if not (isinstance(u, int) and u < 2):
                    sp.wait_ge(wlo_ready, u - 1)
                dst = raw[slot][:].rearrange("p (k n) -> p k n", k=source.shape[1])
                sp.dma_start(dst, source).then_inc(raw_loaded[slot], 16)

            load(0, 0, columns(w_in, 0, C_DT))
            load(1, 1, columns(w_in, 0, C_AG))
            for j in range(12):
                load(U_KV + j, j % 2, columns(w_in, 0, C_KV + P * j))
                if j == 1:
                    for i, name in enumerate(("w_cmp_k1", "w_cmp_v1")):
                        sp.dma_start(w1c[:, i], a[name][0].rearrange("(j p) n -> p j n", p=P)).then_inc(cmpw_loaded, 16)
                    for i, name in enumerate(("w_cmp_k2", "w_cmp_v2")):
                        for e in range(2):
                            sp.dma_start(w2c[:, i, :, e, :],
                                         a[name][0].rearrange("(j p) n -> p j n", p=P)).then_inc(cmpw_loaded, 16)

            with sp.Fori(0, 2) as rr:
                for j in range(4):
                    pp, r2 = divmod(j, 2)
                    u = rr * 4 + (U_Q + j)
                    sp.wait_ge(wlo_ready, u - 1)
                    dst = raw[j % 2][:].rearrange("p (k e n) -> p k e n", k=KT, e=2)
                    for e in range(2):
                        head = rr * 2 + ((2 * pp + e) * R + r2)
                        sp.dma_start(dst[:, :, e, :], columns(w_in, 0, head * HD + C_Q, HD)).then_inc(raw_loaded[j % 2], 16)

            with sp.Fori(1, GROUPS + 1) as after:
                for j, (width, col) in enumerate(((256, C_XS), (256, C_XS + P), (P, C_B), (P, C_C),
                                                  (256, C_Z), (256, C_Z + P))):
                    load(after * 6 + (U_SSM - 6 + j), j % 2, columns(w_in, 0, after * width + (col - width)))
            with sp.Fori(1, 5) as after:
                for t in range(2):
                    col = after * 256 + (t * P - 256)
                    for i, (weight, row0, c0) in enumerate(((w_in, 0, C_MIX), (w_in, 0, C_MIX + D),
                                                            (a["w_attn_branch"][0], 0, 0),
                                                            (a["w_ssm_branch"][0], 0, 0), (a["w_ssm_branch"][0], D, 0))):
                        j = 5 * t + i
                        load(after * 10 + (U_MIX - 10 + j), j % 2, columns(weight, row0, col + c0))

            def rows(weight, row, half):
                return weight[bass.ds(row, 2 * P), half * 512:(half + 1) * 512].rearrange("(k p) n -> p k n", p=P)

            for j in range(8):
                load(U_WO + j, j % 2, rows(a["w_o"][0], (j % 4) * 2 * P, j // 4))
                if j == 2:
                    sp.wait_ge(unit_done, U_WO)
                    sp.dma_start(x1[:], a["x"][0].rearrange("(c p) n -> p c n", p=P)).then_inc(x1_loaded, 16)
                    sp.dma_start(gfin[:], a["g_norm_final"].rearrange("(a n) -> a n", a=1).to_broadcast([P, D])).then_inc(gfin_loaded, 16)
            with sp.Fori(0, 4) as q:
                for j in range(8):
                    load(q * 16 + (U_MLP + j), j % 2, columns(a["w_up"][0], 0, q * D + j * P))
                for j in range(8):
                    load(q * 16 + (U_MLP + 8 + j), j % 2, rows(a["w_down"][0], q * D + (j % 4) * 2 * P, j // 4))
            for n, c in enumerate(DOWN_ORDER):
                sp.wait_ge(out_first, n + 1)
                sp.wait_ge(out_ready, n + 1)
                sp.dma_start(out[0, c * P:(c + 1) * P, :], xn2[:, c, :]).then_inc(out_stored, 16)
            sp.wait_ge(out_stored, 16 * NC)

        def loaded(u):
            return 16 * (u // 2 + 1)

        KV_LANDED = loaded(U_Q - 1)
        SSM_LANDED = KV_LANDED + 128 + 16
        MIX_LANDED = SSM_LANDED + 16 * 3 * GROUPS
        WO_LANDED = MIX_LANDED + 16 * 20
        MLP_LANDED = WO_LANDED + 16 * 4
        Z_READ = U_Q // 2 + 1

        @block.gpsimd
        def _(pool):
            nc.gpsimd.memset(ones[:], 1.0).then_inc(ones_set, 1)
            nc.gpsimd.memset(mean_ssm[:], GROUPS / D_INNER).then_inc(ones_set, 1)
            nc.gpsimd.memset(eps_col[:], EPS).then_inc(ones_set, 1)

            def low(slot):
                nc.gpsimd.tensor_tensor(wlo[slot][:], raw[slot][:], whi[slot][:].bitcast(F32),
                                        ALU.subtract).then_inc(wlo_ready, 1)

            with pool.Fori(0, U_Q // 2 + 1) as pair:
                for slot in range(2):
                    pool.wait_ge(whi_ready, pair * 2 + (slot + 1))
                    low(slot)
            pool.wait_ge(sin_ready, 2)
            with pool.Fori(0, 2) as rr:
                for j in range(4):
                    if j < 2:
                        pool.wait_ge(whi_ready, rr * 4 + (U_Q + 2 + j + 1))
                        low(j % 2)
                    pool.wait_ge(q_copied, rr * 4 + (j + 1))
                    if j >= 2:
                        pool.wait_ge(qlo_ready, rr * 8 + (2 * j - 2))
                    nc.gpsimd.tensor_tensor(vtmp[:, j % 2, :], q_s[:, j, :], ropeC[:], ALU.mult).then_inc(q_cos_ready, 1)
                    if j >= 2:
                        pool.wait_ge(whi_ready, rr * 4 + (U_Q + 2 + j + 1))
                        low(j % 2)
                pool.wait_ge(wlo_ready, rr * 4 + (U_Q + 6))
                for j in (2, 3):
                    for e in range(2):
                        rows = slice(e * HD, (e + 1) * HD)
                        pool.wait_ge(qlo_ready, rr * 8 + (2 * j + e))
                        pool.wait_ge(qhi_ready, rr * 8 + (2 * j + e + 1))
                        nc.gpsimd.tensor_tensor(q_hl[(1 - e) * HD:(2 - e) * HD, 2 * j + e, :], vtmp[rows, j % 2, :],
                                                q_hl[rows, 2 * j + e, :].bitcast(F32), ALU.subtract).then_inc(qlo_ready, 1)
                pool.wait_ge(qlo_ready, rr * 8 + 8)
            with pool.Fori(U_Q // 2 + 5, UNITS // 2) as pair:
                for slot in range(2):
                    pool.wait_ge(whi_ready, pair * 2 + (slot + 1))
                    low(slot)

        @block.scalar
        def _(act):
            def split(u, slot, landed):
                act.wait_ge(raw_loaded[slot], landed)
                if not (isinstance(u, int) and u < 2):
                    act.wait_ge(unit_done, u - 1)
                nc.scalar.activation(whi[slot][:], raw[slot][:], ACT.Copy).then_inc(whi_ready, 1)

            act.wait_ge(ones_set, 3)
            nc.scalar.activation(stat[:, 4:5], eps_col[:, 0:1], ACT.Sqrt)
            for c in range(NC):
                act.wait_ge(x_loaded[c], 16)
                if c:
                    act.wait_ge(sumsq_ready, c)
                nc.scalar.activation(sq_junk[:], x_sb[:, c, :], ACT.Square,
                                     accum_out=stat[:, c:c + 1]).then_inc(sumsq_ready, 1)
                act.wait_ge(sumsq_ready, c + 1)
                nc.scalar.activation(stat[:, 8 + c:9 + c], stat[:, c:c + 1], ACT.Sqrt, scale=1.0 / D,
                                     bias=eps_col[:, 0:1]).then_inc(rms_ready, 1)
            split(0, 0, 16)
            act.wait_ge(vec_ready, 1)
            for k in range(KT):
                act.wait_ge(xn_turned, k + 1)
                nc.scalar.activation(h_hi[:, k, :], h_bank(k)[:], ACT.Copy,
                                     scale=vt[:, V_GMIX + k:V_GMIX + k + 1]).then_inc(hhi_ready, 1)
                if k == 3:
                    split(1, 1, 16)
            act.wait_ge(angle_ready, 1)
            nc.scalar.activation(ropeS[:], rt[:, 0, :], ACT.Sin).then_inc(sin_ready, 1)
            act.wait_ge(angle_ready, 2)
            nc.scalar.activation(ropeC[:], rt[:, 1, :], ACT.Sin).then_inc(sin_ready, 1)
            act.wait_ge(unit_done, 1)
            split(2, 0, loaded(2))
            act.wait_ge(small_loaded, 64)
            nc.scalar.activation(small[:, 2:3], small[:, 1:2], ACT.Exp).then_inc(dt_exp, 1)
            act.wait_ge(dt_neg, 1)
            nc.scalar.activation(dtw[:, 2, :], dtw[:, 1, :], ACT.Exp).then_inc(dt_exp, 1)
            act.wait_ge(dt_one, 1)
            nc.scalar.activation(dtw[:, 4, :], dtw[:, 3, :], ACT.Ln).then_inc(dt_log, 1)
            split(3, 1, loaded(3))
            nc.scalar.activation(ag[:], bank[1][0:48, :], ACT.Sigmoid).then_inc(unit_read[1], 1)
            for j in range(12):
                u = U_KV + j
                if j < 10:
                    split(u + 2, j % 2, loaded(u + 2))
                else:
                    split(u + 2, j % 2, KV_LANDED + 32)
                if j in (6, 10):
                    i = j // 10
                    act.wait_ge(hid_summed, i + 1)
                    act.wait_ge(hid_zeroed, 1)
                    nc.scalar.activation(hid[:, i, :, :, 0:CMP],
                                         bank[2 + i][:, 0:256].rearrange("p (h g k) -> p h g k", h=2, k=32)[:, :, :, 0:CMP],
                                         ACT.Silu).then_inc(hid_ready, 1)
                kind, pp = divmod(j, 2)
                if kind in (3, 5):
                    b = kind // 4
                    act.wait_ge(unit_done, u + 1)
                    if b or pp:
                        act.wait_ge(v_turned, 2 * b + pp)
                    nc.scalar.activation(vtmp[:, pp, :], bank[u % 2][:], ACT.Copy).then_inc(unit_read[u % 2], 1)
                    act.wait_ge(v_turned, 2 * b + pp + 1)
                    nc.scalar.activation(vtok[:, b, :, pp * P:(pp + 1) * P],
                                         bank[4 + pp][:].rearrange("p (c n) -> p c n", c=NC),
                                         ACT.Copy).then_inc(v_ready, 1)
                if j == 4:
                    act.wait_ge(dec_summed, 1)
                    nc.scalar.activation(decs[:].rearrange("p a c h -> p (a c h)"), bank[3][:, 0:256],
                                         ACT.Exp).then_inc(dec_ready, 1)

            for b in (1, 0):
                act.wait_ge(k_ready, 2 * b + 2)
                if b:
                    act.wait_ge(blk_ready, 32)
                else:
                    act.wait_ge(kvc_summed, 2)
                for e in range(2):
                    for to in (e, 1 - e):
                        nc.scalar.activation(kk[b][0][to * HD:(to + 1) * HD, e:KVG:2, :], kT[e * HD:(e + 1) * HD, b, :, :],
                                             ACT.Copy).then_inc(kkhi_ready, 1)

            with act.Fori(0, 2) as rr:
                def high_q(j):
                    act.wait_ge(q_ready, rr * 4 + (j + 1))
                    for e in range(2):
                        rows = slice(e * HD, (e + 1) * HD)
                        nc.scalar.activation(q_hl[rows, 2 * j + e, :], vtmp[rows, j % 2, :], ACT.Copy).then_inc(qhi_ready, 1)

                for j in range(4):
                    act.wait_ge(unit_done, rr * 4 + (U_Q + j + 1))
                    act.wait_ge(raw_loaded[j % 2], rr * 64 + (KV_LANDED + 64) if j < 2 else rr * 48 + (KV_LANDED + 96))
                    nc.scalar.activation(whi[j % 2][:], raw[j % 2][:], ACT.Copy).then_inc(whi_ready, 1)
                    nc.scalar.activation(q_s[:, j, :], bank[j % 2][:], ACT.Copy,
                                         scale=float(HD) ** -0.5).then_inc(q_copied, 1)
                    if j == 2:
                        high_q(0)
                        high_q(1)

                def cmp_exp(i):
                    act.wait_ge(cs_centred, rr * NC + (i + 1))
                    nc.scalar.activation(cp[:, 1], cp[:, 0], ACT.Exp).then_inc(cs_exp, 1)

                def exp(n):
                    act.wait_ge(max_ready, rr * 64 + (n + 1))
                    if n >= 4:
                        act.wait_ge(prob_turned, rr * 64 + (n - 3))
                    w = (n // 16 + 1) * P
                    nc.scalar.activation(prob[n % 4][:, 0:w], score_bank(n)[:, 0:w], ACT.Exp,
                                         bias=nmax[:, n % 4:n % 4 + 1],
                                         accum_out=esum[:, n % 4:n % 4 + 1]).then_inc(exp_ready, 1)

                def high_out(g4):
                    i, g = divmod(g4, KVG)
                    act.wait_ge(pv_done, rr * 64 + (4 * g4 + 4))
                    nc.scalar.activation(o_hi[:, bass.ds(rr + 2 * g, 1), i * P:(i + 1) * P],
                                         bank[6 + g % 2][:, 0:P], ACT.Copy).then_inc(ohi_ready, 1)

                def copy_cmp(n, i, t):
                    act.wait_ge(cp_turned, rr * 8 + (2 * i + t + 1))
                    nc.scalar.activation(pcT[i % 2][:, t, :], bank[4 + n % 2][:, 3 * P:S], ACT.Copy).then_inc(pcT_ready, 1)

                exp(0)
                exp(1)
                exp(2)
                for n in range(64):
                    w = (n // 16 + 1) * P
                    act.wait_ge(prob_turned, rr * 64 + (n + 1))
                    if n >= 2:
                        act.wait_ge(pv_done, rr * 64 + (n - 1))
                    nc.scalar.activation(pT[n % 2][:, 0:w], bank[4 + n % 2][:, 0:w], ACT.Copy).then_inc(pT_ready, 1)
                    if n in (1, 3):
                        high_q(2 + n // 3)
                    if cmp_turned(n):
                        copy_cmp(n, *cmp_turned(n))
                    if n + 3 < 64:
                        exp(n + 3)
                    if n == 0:
                        cmp_exp(0)
                    if n % 16 == 6 and n < 48:
                        cmp_exp(n // 16 + 1)
                    if n % 4 == 1 and n > 4:
                        high_out(n // 4 - 1)
                high_out(15)

            def split_next(landed, done, slot):
                act.wait_ge(unit_done, done)
                act.wait_ge(raw_loaded[slot], landed)
                nc.scalar.activation(whi[slot][:], raw[slot][:], ACT.Copy).then_inc(whi_ready, 1)

            def norm_root(g, sums=2):
                act.wait_ge(yms_done, g + 1)
                nc.scalar.activation(rs, bank[sums][:], ACT.Ln, bias=eps_col[:, 0:1]).then_inc(yln_ready, 1)
                act.wait_ge(yln_ready, g + 1)
                nc.scalar.activation(rs, rs, ACT.Exp, scale=-0.5).then_inc(yrs_ready, 1)

            def high_y(g):
                for j in range(2):
                    act.wait_ge(yn_ready, g * 2 + (j + 1))
                    nc.scalar.activation(y_hi[:, bass.ds(g * 2 + j, 1), :], yt[:, j:j + 1, :], ACT.Copy).then_inc(yhi_ready, 1)

            def squares(g):
                for j in range(2):
                    act.wait_ge(y_gated, g * 2 + (j + 1))
                    nc.scalar.activation(sq[:, j, :], yt[:, j, :], ACT.Square).then_inc(ysq_ready, 1)

            def group(g, first):
                def arrive(j):
                    split_next(g * 48 + (SSM_LANDED + 16 * (j // 2 + 1)), g * 6 + (U_SSM + j + 1), j % 2)

                def tile_of(j):
                    return g * 2 + j if j < 2 else g + (16 if j == 2 else 24)

                def conv_first(j):
                    nc.scalar.activation(grp[:, j, :], bank[j % 2][:], ACT.Identity,
                                         scale=vt[:, bass.ds(tile_of(j) + (V_CW + 3 * 32), 1)],
                                         bias=vt[:, bass.ds(tile_of(j) + V_CB, 1)]).then_inc(conv_begun, 1)

                def conv_silu(j):
                    act.wait_ge(conv_summed, g * 4 + (j + 1))
                    nc.scalar.activation(grp[:, j, :], grp[:, j, :], ACT.Silu).then_inc(conv_ready, 1)

                def seg_exp(c):
                    act.wait_ge(seg_summed, g * 4 + (c + 1))
                    nc.scalar.activation(mdec[:, c].rearrange("p h l -> p (h l)"), bank[6 + c % 2][:],
                                         ACT.Exp).then_inc(dec_exp, 1)

                arrive(0)
                if not first:
                    act.wait_ge(ssm_steps, g * 8 - 4)
                conv_first(0)
                if not first:
                    squares(g - 1)
                for j in range(1, 4):
                    arrive(j)
                    conv_first(j)
                    if j == 1 and not first:
                        norm_root(g - 1)
                    seg_exp(j - 1)
                    if j == 1 and not first:
                        high_y(g - 1)
                seg_exp(3)
                for j in range(4):
                    conv_silu(j)
                arrive(4)
                nc.scalar.activation(grp[:, 4, :], bank[0][:], ACT.Silu).then_inc(unit_read[0], 1)
                act.wait_ge(b_turned, g + 1)
                nc.scalar.activation(btok[:].rearrange("p c n -> p (c n)"), bank[4][:], ACT.Copy).then_inc(btok_ready, 1)
                arrive(5)
                nc.scalar.activation(grp[:, 5, :], bank[1][:], ACT.Silu).then_inc(unit_read[1], 1)
                for j in range(2):
                    act.wait_ge(eo_summed, g * 2 + (j + 1))
                    nc.scalar.activation(eo[:, j, :], bank[6 + j][:, P:S], ACT.Exp).then_inc(eo_ready, 1)

            group(0, first=True)
            with act.Fori(1, GROUPS) as g:
                group(g, first=False)
            def mix(m, first):
                for t in range(2):
                    for i in range(5):
                        j = 5 * t + i
                        split_next(m * 80 + (MIX_LANDED + 16 * (j // 2 + 1)), m * 10 + (U_MIX + j + 1), j % 2)
                        if i < 2:
                            nc.scalar.activation(sig[:, i, :], bank[4 * t + i][:], ACT.Sigmoid).then_inc(mix_sig, 1)
                        if first and j == 0:
                            squares(GROUPS - 1)
                        if first and j == 2:
                            norm_root(GROUPS - 1, sums=6)
                            high_y(GROUPS - 1)
                    act.wait_ge(mix_sum, m * 2 + (t + 1))
                    nc.scalar.activation(m_hi[:, bass.ds(m * 2 + t, 1), :], mt[:, 0:1, :], ACT.Copy).then_inc(mhi_ready, 1)

            mix(0, first=True)
            with act.Fori(1, 4) as m:
                mix(m, first=False)

            def square2(i, half, n, c):
                m = NC * half + n
                if m >= 2:
                    act.wait_ge(n2_sumsq[i], m - 1)
                nc.scalar.activation(junk2[:, m % 2, :], x1[:, c, half * 512:half * 512 + 512],
                                     ACT.Square, accum_out=stat2[:, i, 8 * half + c:8 * half + c + 1]).then_inc(n2_sumsq[i], 1)

            def root_table(i):
                nc.scalar.activation(stat2[:, i, 20:21], eps_col[:, 0:1], ACT.Sqrt)

            def second_half(i, order, ready, count, src, sem_to):
                def scale(n):
                    c = order[n]
                    act.wait_ge(n2_rstd[i], n + 1)
                    nc.scalar.activation(xn2[:, c, 0:512], src[:, c, 0:512], ACT.Copy,
                                         scale=stat2[:, i, 12 + c:13 + c]).then_inc(sem_to, 1)

                act.wait_ge(n2_pre[i], 1)
                for n, c in enumerate(order):
                    act.wait_ge(ready, count + (n + 1))
                    square2(i, 1, n, c)
                    act.wait_ge(n2_sumsq[i], NC + (n + 1))
                    nc.scalar.activation(stat2[:, i, 16 + c:17 + c], stat2[:, i, 8 + c:9 + c], ACT.Sqrt,
                                         scale=1.0 / D, bias=stat2[:, i, 4 + c:5 + c]).then_inc(n2_rms[i], 1)
                    if n:
                        scale(n - 1)
                scale(NC - 1)

            def split_wo(j):
                split_next(WO_LANDED + 16 * (j // 2 + 1), U_WO + j + 1, j % 2)

            for j in range(7):
                split_wo(j)
                if j == 4:
                    for n, c in enumerate(WO_ORDER):
                        act.wait_ge(x1_ready, n + 1)
                        square2(0, 0, n, c)
                    root_table(0)
            second_half(0, WO_ORDER, x1_ready, NC, x1, xn2_first)
            for k in range(KT):
                act.wait_ge(xn2_turned, k + 1)
                nc.scalar.activation(h_hi[:, k, :], h2_bank(k)[:], ACT.Copy,
                                     scale=vt[:, V_GMLP + k:V_GMLP + k + 1]).then_inc(h2hi_ready, 1)
                if k == 3:
                    split_wo(7)

            def quarter(q, last):
                def split_mlp(j):
                    split_next(q * 128 + (MLP_LANDED + 16 * (j // 2 + 1)), q * 16 + (U_MLP + j + 1), j % 2)

                for j in range(9):
                    if j < 8:
                        split_mlp(j)
                        nc.scalar.activation(rel[:, j % 2, :], bank[2 + j % 2][:], ACT.Relu).then_inc(relu_ready, 1)
                    if j:
                        act.wait_ge(uf_ready, q * 8 + j)
                        nc.scalar.activation(u_hi[:, j - 1, :], uf[:, (j - 1) % 2, :], ACT.Copy).then_inc(uhi_ready, 1)
                for j in range(8, 14 if last else 16):
                    split_mlp(j)
                    if last and j == 12:
                        for n, c in enumerate(DOWN_ORDER):
                            act.wait_ge(down_added, 4 + 3 * 2 * NC + (n + 1))
                            square2(1, 0, n, c)
                        root_table(1)

            with act.Fori(0, 3) as q:
                quarter(q, last=False)
            quarter(3, last=True)
            act.wait_ge(xg_ready, NC)
            second_half(1, DOWN_ORDER, down_added, 4 + 3 * 2 * NC + NC, xn2, out_first)


        @block.vector
        def _(dve):
            step = Steps(dve, dve_steps)
            V = nc.vector

            dve.wait_ge(const_loaded, 16)
            V.tensor_copy(ident_bf[:], ident).then_inc(masks_ready, 1)
            V.tensor_copy(causal_bf[:], cst[:, K_CB:K_CB + P]).then_inc(masks_ready, 1)

            for c in range(NC):
                dve.wait_ge(rms_ready, c + 1)
                V.reciprocal(stat[:, 12 + c:13 + c], stat[:, 8 + c:9 + c]).then_inc(rstd_ready, 1)
                dve.wait_ge(rstd_ready, c + 1)
                V.tensor_scalar(xn[:, c, :], x_sb[:, c, :], stat[:, 12 + c:13 + c], None,
                                ALU.mult).then_inc(xn_ready, 1)
            dve.wait_ge(vec_turned, 1)
            V.tensor_copy(vt[:], bank[2][:, 0:240]).then_inc(vec_ready, 1)
            dve.wait_ge(vec_ready, 1)
            for k in range(KT):
                dve.wait_ge(hhi_ready, k + 1)
                V.scalar_tensor_tensor(h_lo[:, k, :], h_bank(k)[:], vt[:, V_GMIX + k:V_GMIX + k + 1],
                                       h_hi[:, k, :].bitcast(F32), ALU.mult, ALU.subtract).then_inc(hlo_ready, 1)

            dve.wait_ge(small_loaded, 64)
            step(V.tensor_copy(rt[:, 0, :], pos_i[:]))
            step.wait()
            step(V.tensor_scalar(rt[:, 1, :], rt[:, 0, :], cst[:, K_F:K_F + 1], None, ALU.mult))
            step.wait()
            step(V.tensor_scalar(rt[:, 2, :], rt[:, 1, :], 1.0 / TWO_PI, None, ALU.mult))
            step.wait()
            step(V.tensor_scalar(rt[:, 0, :], rt[:, 2, :], MAGIC, None, ALU.add))
            step.wait()
            step(V.tensor_scalar(rt[:, 2, :], rt[:, 0, :], MAGIC, None, ALU.subtract))
            for n, part in enumerate((PI_A, PI_B, PI_C)):
                step.wait()
                step(V.scalar_tensor_tensor(rt[:, n % 2, :], rt[:, 2, :], -part, rt[:, 1 - n % 2, :],
                                            ALU.mult, ALU.add))
            step.wait()
            step(V.tensor_scalar(rt[:, 1, :], rt[:, 0, :], np.pi / 2, None, ALU.add))
            step(V.tensor_scalar(rt[:, 2, :], rt[:, 0, :], np.pi / 2, None, ALU.is_gt))
            step.wait()
            V.tensor_scalar(rt[:, 0, :], rt[:, 0, :], -SIN_MAX, SIN_MAX, ALU.max, ALU.min).then_inc(angle_ready, 1)
            step(V.scalar_tensor_tensor(rt[:, 1, :], rt[:, 2, :], -TWO_PI, rt[:, 1, :], ALU.mult, ALU.add))
            step.wait()
            V.tensor_scalar(rt[:, 1, :], rt[:, 1, :], -SIN_MAX, SIN_MAX, ALU.max, ALU.min).then_inc(angle_ready, 1)
            dve.wait_ge(sin_ready, 2)
            V.tensor_scalar(ropeS[:], ropeS[:], cst[:, K_F + 1:K_F + 2], None, ALU.mult).then_inc(rope_ready, 1)

            dve.wait_ge(unit_done, 1)
            V.tensor_scalar(dtw[:, 0, :], bank[0][0:HEADS, :], small[:, 0:1], None, ALU.add).then_inc(unit_read[0], 1)
            dve.wait_ge(unit_read[0], 1)
            V.scalar_tensor_tensor(dtw[:, 1, :], dtw[:, 0, :], -1.0, dtw[:, 0, :],
                                   ALU.mult, ALU.min).then_inc(dt_neg, 1)
            dve.wait_ge(dt_exp, 2)
            V.tensor_scalar(dtw[:, 3, :], dtw[:, 2, :], 1.0, None, ALU.add).then_inc(dt_one, 1)
            dve.wait_ge(dt_one, 1)
            step(V.tensor_scalar(dtw[:, 5, :], dtw[:, 3, :], 1.0, None, ALU.subtract))
            step.wait()
            step(V.tensor_scalar(dtw[:, 6, :], dtw[:, 5, :], 0.0, None, ALU.is_equal))
            step.wait()
            step(V.tensor_tensor(dtw[:, 5, :], dtw[:, 5, :], dtw[:, 6, :], ALU.add))
            dve.wait_ge(dt_log, 1)
            step(V.tensor_tensor(dtw[:, 7, :], dtw[:, 4, :], dtw[:, 6, :], ALU.add))
            step.wait()
            step(V.reciprocal(dtw[:, 3, :], dtw[:, 5, :]))
            step.wait()
            step(V.tensor_tensor(dtw[:, 7, :], dtw[:, 7, :], dtw[:, 3, :], ALU.mult))
            step.wait()
            step(V.tensor_tensor(dtw[:, 7, :], dtw[:, 7, :], dtw[:, 2, :], ALU.mult))
            step.wait()
            V.scalar_tensor_tensor(dtw[:, 1, :], dtw[:, 0, :], 0.0, dtw[:, 7, :], ALU.max, ALU.add).then_inc(dt_ready, 1)
            dve.wait_ge(dt_ready, 1)
            V.tensor_scalar(dtw[:, 4, :], dtw[:, 1, :], small[:, 2:3], -1.0, ALU.mult, ALU.mult).then_inc(dt_ready, 1)

            def blocks(i):
                if i == 0:
                    V.memset(hid[:], 0.0).then_inc(hid_zeroed, 1)
                    V.memset(kc[:], 0.0).then_inc(hid_zeroed, 1)
                else:
                    dve.wait_ge(hid_summed, 1)
                for jj in range(16):
                    V.tensor_scalar(blk[:, jj, 0:KVG * CMP].rearrange("p (g k) -> p g k", g=KVG),
                                    kcx[:, i, :, 2 * jj:2 * jj + 16 * (CMP - 1) + 1:16],
                                    vt[:, V_PE + 16 * i + jj:V_PE + 16 * i + jj + 1], None,
                                    ALU.add).then_inc(blk_ready, 1)

            for j in range(12):
                u = U_KV + j
                kind, pp = divmod(j, 2)
                if kind < 2:
                    dve.wait_ge(unit_done, u + 1)
                    for e in range(2):
                        src = bank[u % 2][e * HD:(e + 1) * HD, :]
                        step(V.tensor_copy(kcx[0:HD, kind, 2 * pp + e, :], src))
                        ins = V.tensor_copy(kcx[HD:P, kind, 2 * pp + e, 0:S - 1], src[:, 1:S])
                        if e == 0:
                            step(ins)
                        else:
                            ins.then_inc(unit_read[u % 2], 1)
                elif kind in (2, 4):
                    b = kind // 4
                    dve.wait_ge(unit_done, u + 1)
                    V.tensor_copy(kT[:, b, pp, :], bank[u % 2][:]).then_inc(unit_read[u % 2], 1)
                    if pp == 0:
                        blocks(b)
                    dve.wait_ge(k_swapped, 2 * b + pp + 1)
                    dve.wait_ge(rope_ready, 1)
                    if b or pp:
                        dve.wait_ge(k_ready, 2 * b + pp)
                    step(V.tensor_tensor(rtmp[:], bank[6 + pp][:], ropeS[:], ALU.mult))
                    step(V.tensor_tensor(kT[:, b, pp, :], kT[:, b, pp, :], ropeC[:], ALU.mult))
                    step.wait()
                    V.tensor_tensor(kT[:, b, pp, :], kT[:, b, pp, :], rtmp[:], ALU.add).then_inc(k_ready, 1)
                if j == 1:
                    dve.wait_ge(dt_turned, 1)
                    V.tensor_copy(dtT[:].rearrange("p a c h -> p (a c h)"), bank[2][:, 0:256]).then_inc(dtT_ready, 1)
                if j == 2:
                    dve.wait_ge(ag_turned, 1)
                    V.tensor_copy(gate[:].rearrange("p c n -> p (c n)"), bank[4][:, 0:192]).then_inc(gate_ready, 1)
                if j == 4:
                    dve.wait_ge(dec_ready, 1)
                    step(V.tensor_tensor(dd[:], dtT[:, 0], decs[:, 0], ALU.mult))
                    V.tensor_copy(stri_r[:], stri).then_inc(dta_split, 1)
                    V.tensor_copy(dta_parts[:, 0], dtT[:, 1]).then_inc(dta_split, 1)
                    dve.wait_ge(dta_split, 2)
                    V.tensor_tensor(dta_parts[:, 1], dtT[:, 1], dta_parts[:, 0].bitcast(F32),
                                    ALU.subtract).then_inc(dta_split, 1)

                if j == 8:
                    dve.wait_ge(kvc_summed, 1)
                    dve.wait_ge(hid_zeroed, 2)
                    for e in range(2):
                        V.tensor_copy(kc[e * HD:(e + 1) * HD, :, 32 * e:32 * e + 32],
                                      bank[2][e * HD:(e + 1) * HD, 0:P].rearrange("p (m e k) -> p m e k", m=2, e=2)[:, :, e],
                                      ).then_inc(kvc_ready, 1)
                if j == 10:
                    dve.wait_ge(hid_ready, 2)
                    hv = hid[:, 1].rearrange("p h g k -> p (h g) k")
                    V.tensor_copy(hidr[:].rearrange("p h g e k -> p (h g) e k"),
                                  hv.unsqueeze(2).to_broadcast([P, 8, 4, 32])).then_inc(hidr_ready, 1)
                    step(V.tensor_scalar(cbias[:], cmask, -1.0, -NEG, ALU.add, ALU.mult))
            dve.wait_ge(kvc_summed, 2)
            V.tensor_copy(vc[:].rearrange("p g d -> p (g d)"), bank[3][:, 0:256]).then_inc(kvc_ready, 1)
            step.wait()

            for n, b in enumerate((1, 0)):
                for e in range(2):
                    rows = slice(e * HD, (e + 1) * HD)
                    dve.wait_ge(kkhi_ready, 4 * n + 2 * e + 2)
                    for to in (e, 1 - e):
                        V.tensor_tensor(kk[b][1][to * HD:(to + 1) * HD, e:KVG:2, :], kT[rows, b, :, :],
                                        kk[b][0][rows, e:KVG:2, :].bitcast(F32), ALU.subtract).then_inc(kklo_ready, 1)

            with dve.Fori(0, 2) as rr:
                step.loop(rr, 4 + 4 * 5 + 64)

                def rope_q(j):
                    dve.wait_ge(q_swapped, rr * 4 + (j + 1))
                    if j:
                        dve.wait_ge(q_ready, rr * 4 + j)
                    roped = vtmp[:, j % 2, :]
                    step(V.tensor_tensor(rtmp[:], bank[6 + j % 2][:], ropeS[:], ALU.mult))
                    dve.wait_ge(q_cos_ready, rr * 4 + (j + 1))
                    step.wait()
                    V.tensor_tensor(roped, roped, rtmp[:], ALU.add).then_inc(q_ready, 1)

                def low_q(j):
                    for e in range(2):
                        rows = slice(e * HD, (e + 1) * HD)
                        dve.wait_ge(qhi_ready, rr * 8 + (2 * j + e + 1))
                        V.tensor_tensor(q_hl[(1 - e) * HD:(2 - e) * HD, 2 * j + e, :], vtmp[rows, j % 2, :],
                                        q_hl[rows, 2 * j + e, :].bitcast(F32), ALU.subtract).then_inc(qlo_ready, 1)

                def cmp_read(pp):
                    dve.wait_ge(cs_ready, rr * 2 + (pp + 1))
                    for e in range(2):
                        V.tensor_tensor(cs[:, e, :, 2 * pp:2 * pp + 2],
                                        bank[4 + pp][:].rearrange("p (i h e k) -> p i h e k", i=NC, e=2, k=32)[:, :, :, e],
                                        cbias[:].unsqueeze(2).to_broadcast([P, NC, 2, 32]),
                                        ALU.add).then_inc(cs_read, 1)

                def cmp_centre(i):
                    dve.wait_ge(cs_read, rr * 4 + 4)
                    if i:
                        dve.wait_ge(cp_turned, rr * 8 + 2 * i)
                    step(V.tensor_reduce(cst8[:, 3, :].rearrange("p (e h) -> p e h", e=2), cs[:, :, i], AX.X, ALU.max))
                    step.wait()
                    V.tensor_tensor(cp[:, 0].rearrange("p (e h) k -> p e h k", e=2), cs[:, :, i],
                                    cst8[:, 3, :].rearrange("p (e h) -> p e h", e=2).unsqueeze(3).to_broadcast([P, 2, 4, 32]),
                                    ALU.subtract).then_inc(cs_centred, 1)

                def cmp_probs(i):
                    dve.wait_ge(cs_exp, rr * NC + (i + 1))
                    step(V.tensor_reduce(cst8[:, 0, :], cp[:, 1], AX.X, ALU.add))
                    step(V.tensor_tensor(cp[:, 0], cp[:, 1], cmask[:, i, :].unsqueeze(1).to_broadcast([P, 8, 32]),
                                         ALU.mult))
                    step.wait()
                    step(V.reciprocal(cst8[:, 1, :], cst8[:, 0, :]))
                    step.wait()
                    gates = gate[:, i, 0:16].rearrange("p (m e r) -> p e m r", m=2, e=2)[:, :, :, bass.ds(rr * 2, 2)]
                    step(V.tensor_tensor(cst8[:, 2, :].rearrange("p (e m r) -> p e m r", e=2, m=2),
                                         cst8[:, 1, :].rearrange("p (e m r) -> p e m r", e=2, m=2), gates, ALU.mult))
                    step.wait()
                    V.tensor_tensor(cp[:, 2], cp[:, 0], cst8[:, 2, :].unsqueeze(2).to_broadcast([P, 8, 32]),
                                    ALU.mult).then_inc(cp_ready, 1)

                def row_max(n):
                    dve.wait_ge(s_ready, rr * 64 + (n + 1))
                    w = (n // 16 + 1) * P
                    V.tensor_reduce(nmax[:, n % 4:n % 4 + 1], score_bank(n)[:, 0:w], AX.X, ALU.max,
                                    negate=True).then_inc(max_ready, 1)

                def over_sum(n):
                    dve.wait_ge(exp_ready, rr * 64 + (n + 1))
                    step(V.reciprocal(rsum[:, n % 4:n % 4 + 1], esum[:, n % 4:n % 4 + 1]))

                def scale_probs(n):
                    i, b = divmod(n, 16)
                    g, r2, br = b // 4, b // 2 % 2, b % 2
                    w = (i + 1) * P
                    step.wait()
                    V.tensor_scalar(prob[n % 4][:, 0:w], prob[n % 4][:, 0:w], rsum[:, n % 4:n % 4 + 1],
                                    gate[:, i, bass.ds(rr * 2 + (16 * (br + 1) + g * R + r2), 1)],
                                    ALU.mult, ALU.mult).then_inc(prob_ready, 1)

                def low_out(g4):
                    i, g = divmod(g4, KVG)
                    dve.wait_ge(ohi_ready, rr * 16 + (g4 + 1))
                    where = (slice(None), bass.ds(rr + 2 * g, 1), slice(i * P, (i + 1) * P))
                    V.tensor_tensor(o_lo[where], bank[6 + g % 2][:, 0:P].unsqueeze(1), o_hi[where].bitcast(F32),
                                    ALU.subtract).then_inc(olo_ready, 1)

                rope_q(0)
                rope_q(1)
                low_q(0)
                low_q(1)
                cmp_read(0)
                rope_q(2)
                row_max(0)
                row_max(1)
                row_max(2)
                over_sum(0)
                for n in range(64):
                    scale_probs(n)
                    if n + 1 < 64:
                        over_sum(n + 1)
                    if n + 3 < 64:
                        row_max(n + 3)
                    if n == 0:
                        cmp_read(1)
                        cmp_centre(0)
                    if n == 1:
                        rope_q(3)
                    if n == 2:
                        cmp_probs(0)
                    if n < 48 and n % 16 == 5:
                        cmp_centre(n // 16 + 1)
                    if n < 48 and n % 16 == 8:
                        cmp_probs(n // 16 + 1)
                    if n % 4 == 2 and n > 4:
                        low_out(n // 4 - 1)
                low_out(15)
                step.end(2)

            def norm_tail(g):
                dve.wait_ge(y_gated, g * 2 + 2)
                dve.wait_ge(yrs_ready, g + 1)
                for j in range(2):
                    V.scalar_tensor_tensor(yt[:, j, :], yt[:, j, :], vt[:, bass.ds(g * 2 + (V_GSSM + j), 1)], rs,
                                           ALU.mult, ALU.mult).then_inc(yn_ready, 1)
                for j in range(2):
                    where = bass.ds(g * 2 + j, 1)
                    dve.wait_ge(yhi_ready, g * 2 + (j + 1))
                    dve.wait_ge(yn_ready, g * 2 + (j + 1))
                    V.tensor_tensor(y_lo[:, where, :], yt[:, j:j + 1, :], y_hi[:, where, :].bitcast(F32),
                                    ALU.subtract).then_inc(ylo_ready, 1)

            steps = Steps(dve, ssm_steps)
            dve.wait_ge(dta_split, 3)

            def gated(g):
                for j in range(2):
                    dve.wait_ge(eo_ready, g * 2 + (j + 1))
                    dve.wait_ge(yo_done, g * 2 + (j + 1))
                    steps(V.tensor_tensor(eo[:, j, :], bank[4 + j][:, P:S], eo[:, j, :], ALU.mult))
                    steps.wait()
                    steps(V.tensor_tensor(yt[:, j, P:S], yt[:, j, P:S], eo[:, j, :], ALU.add))
                    dve.wait_ge(unit_read[j], g + Z_READ)
                    steps.wait()
                    V.tensor_tensor(yt[:, j, :], yt[:, j, :], grp[:, 4 + j, :], ALU.mult).then_inc(y_gated, 1)

            def group(g, first):
                steps.n, steps.base = 0, 0 if first else g * 8 - 4
                heads = bass.ds(g * HPG, HPG)

                def seg_operand(c):
                    if c or not first:
                        dve.wait_ge(seg_summed, g * 4 + c)
                    for part, to in enumerate((seg_hi, seg_lo)):
                        V.tensor_tensor(to[:], tri.unsqueeze(1).to_broadcast([P, HPG, P]),
                                        dta_parts[:, part, c, heads].bitcast(F32).unsqueeze(2).to_broadcast([P, HPG, P]),
                                        ALU.mult).then_inc(segr_ready, 1)

                def conv(j):
                    tile = g * 2 + j if j < 2 else g + (16 if j == 2 else 24)
                    dve.wait_ge(conv_begun, g * 4 + (j + 1))
                    for back in range(1, CONV):
                        ins = V.scalar_tensor_tensor(
                            grp[:, j, back:S], bank[j % 2][:, 0:S - back],
                            vt[:, bass.ds(tile + (V_CW + (CONV - 1 - back) * 32), 1)],
                            grp[:, j, back:S], ALU.mult, ALU.add)
                        if back < CONV - 1:
                            ins.then_inc(conv_step, 1)
                            dve.wait_ge(conv_step, g * 8 + (j * 2 + back))
                        else:
                            ins.then_inc(conv_summed, 1)

                seg_operand(0)
                if not first:
                    gated(g - 1)
                conv(0)
                seg_operand(1)
                conv(1)
                seg_operand(2)
                if not first:
                    norm_tail(g - 1)
                V.tensor_copy(dtab[:].rearrange("p c (h d) -> p c h d", h=HPG),
                              dtT[:, 1, 1:NC, heads].unsqueeze(3).to_broadcast([P, NC - 1, HPG, HD])).then_inc(dtab_ready, 1)
                conv(2)
                seg_operand(3)
                conv(3)
                for n in range(2):
                    dve.wait_ge(x_turned, g * 2 + (n + 1))
                    src = bank[2 + n][:].rearrange("p (c h d) -> p c h d", c=2, h=HPG)
                    V.tensor_tensor(xdt[:, 2 * n:2 * n + 2].rearrange("p c (h d) -> p c h d", h=HPG), src,
                                    dtT[:, 0, 2 * n:2 * n + 2, heads].unsqueeze(3).to_broadcast([P, 2, HPG, HD]),
                                    ALU.mult).then_inc(xdt_ready, 1)
                    w = 2 - n
                    V.tensor_tensor(xdd[:, 2 * n:2 * n + w].rearrange("p c (h d) -> p c h d", h=HPG), src[:, 0:w],
                                    dd[:, 2 * n:2 * n + w, heads].unsqueeze(3).to_broadcast([P, w, HPG, HD]),
                                    ALU.mult).then_inc(xdd_ready, 1)
                dve.wait_ge(cb_done, g + 1)
                V.tensor_tensor(cbm[:], bank[5][:].rearrange("p (c l) -> p c l", c=NC),
                                tri.unsqueeze(1).to_broadcast([P, NC, P]), ALU.mult).then_inc(cbm_ready, 1)
                dve.wait_ge(cbm_ready, g + 1)
                for c in range(NC):
                    dve.wait_ge(dec_exp, g * 4 + (c + 1))
                    V.tensor_tensor(mdec[:, c], mdec[:, c], cbm[:, c, :].unsqueeze(1).to_broadcast([P, HPG, P]),
                                    ALU.mult).then_inc(mdec_ready, 1)
                dve.wait_ge(st_done, g + 1)
                V.tensor_copy(prev[:, 0, :], bank[4][:, 0:256]).then_inc(prev_ready, 1)
                for c in range(1, NC - 1):
                    dve.wait_ge(prev_ready, g * 3 + c)
                    steps(V.tensor_tensor(prev[:, c, :].rearrange("p (h d) -> p h d", h=HPG),
                                          prev[:, c - 1, :].rearrange("p (h d) -> p h d", h=HPG),
                                          decs[:, 1, c, heads].unsqueeze(2).to_broadcast([P, HPG, HD]), ALU.mult))
                    steps.wait()
                    V.tensor_tensor(prev[:, c, :], prev[:, c, :], bank[4 + c // 2][:, (c % 2) * 256:(c % 2) * 256 + 256],
                                    ALU.add).then_inc(prev_ready, 1)
                for j in range(2):
                    dve.wait_ge(yd_done, g * 2 + (j + 1))
                    steps(V.scalar_tensor_tensor(yt[:, j, :], grp[:, j, :], vt[:, bass.ds(g * 2 + (V_D + j), 1)],
                                                 bank[2 + j][:], ALU.mult, ALU.add))
                assert steps.n == (4 if first else 8)

            group(0, first=True)
            with dve.Fori(1, GROUPS) as g:
                group(g, first=False)
            dve.sem_inc(mlo_ready, 2)
            steps.n, steps.base = 0, GROUPS * 8 - 4
            gated(GROUPS - 1)
            norm_tail(GROUPS - 1)
            with dve.Fori(0, 4) as m:
                for t in range(2):
                    dve.wait_ge(mix_sig, m * 4 + (2 * t + 2))
                    dve.wait_ge(mlo_ready, m * 2 + (t + 2))
                    for i, done in ((1, 3), (0, 5)):
                        dve.wait_ge(unit_done, m * 10 + (U_MIX + 5 * t + done))
                        V.tensor_tensor(mt[:, i, :], bank[4 * t + 3 - i][:], sig[:, i, :], ALU.mult).then_inc(mix_part, 1)
                    dve.wait_ge(mix_part, m * 4 + (2 * t + 2))
                    V.tensor_tensor(mt[:, 0, :], mt[:, 0, :], mt[:, 1, :], ALU.add).then_inc(mix_sum, 1)
                    where = bass.ds(m * 2 + t, 1)
                    dve.wait_ge(mhi_ready, m * 2 + (t + 1))
                    V.tensor_tensor(m_lo[:, where, :], mt[:, 0:1, :], m_hi[:, where, :].bitcast(F32),
                                    ALU.subtract).then_inc(mlo_ready, 1)

            dve.sem_inc(down_added, 4)
            dve.wait_ge(x1_loaded, 16)
            def before_roots(i):
                dve.wait_ge(n2_sumsq[i], NC)
                V.tensor_scalar(stat2[:, i, 4:8], stat2[:, i, 0:4], 1.0 / D, EPS, ALU.mult, ALU.add).then_inc(n2_pre[i], 1)

            def one_over(i, n, c):
                dve.wait_ge(n2_rms[i], n + 1)
                V.reciprocal(stat2[:, i, 12 + c:13 + c], stat2[:, i, 16 + c:17 + c]).then_inc(n2_rstd[i], 1)
                dve.wait_ge(n2_rstd[i], n + 1)
                return stat2[:, i, 12 + c:13 + c]

            def normed(n):
                c = WO_ORDER[n]
                V.tensor_scalar(xn2[:, c, 512:D], x1[:, c, 512:D], one_over(0, n, c), None, ALU.mult).then_inc(xn2_ready, 1)

            for half in range(2):
                for n, c in enumerate(WO_ORDER):
                    cols = slice(half * 512, half * 512 + 512)
                    wait_sum(dve, n, 3 * half, U_WO + 4 * half + 4)
                    V.tensor_tensor(x1[:, c, cols], bank[4 * half + c][:], x1[:, c, cols], ALU.add).then_inc(x1_ready, 1)
                    if half and n:
                        normed(n - 1)
                if half == 0:
                    before_roots(0)
            normed(NC - 1)
            for k in range(KT):
                dve.wait_ge(h2hi_ready, k + 1)
                V.scalar_tensor_tensor(h_lo[:, k, :], h2_bank(k)[:], vt[:, V_GMLP + k:V_GMLP + k + 1],
                                       h_hi[:, k, :].bitcast(F32), ALU.mult, ALU.subtract).then_inc(h2lo_ready, 1)

            def final(n):
                c = DOWN_ORDER[n]
                V.scalar_tensor_tensor(xn2[:, c, 512:D], x1[:, c, 512:D], one_over(1, n, c), gfin[:, 512:D],
                                       ALU.mult, ALU.mult).then_inc(out_ready, 1)

            def quarter(q, last):
                for j in range(9):
                    if j < 8:
                        dve.wait_ge(relu_ready, q * 8 + (j + 1))
                        if j >= 2:
                            dve.wait_ge(ulo_ready, q * 8 + (j - 1))
                        V.tensor_tensor(uf[:, j % 2, :], rel[:, j % 2, :], rel[:, j % 2, :], ALU.mult).then_inc(uf_ready, 1)
                    if j:
                        dve.wait_ge(uhi_ready, q * 8 + j)
                        V.tensor_tensor(u_lo[:, j - 1, :], uf[:, (j - 1) % 2, :], u_hi[:, j - 1, :].bitcast(F32),
                                        ALU.subtract).then_inc(ulo_ready, 1)
                for half in range(2):
                    cols = slice(half * 512, half * 512 + 512)
                    for n, c in enumerate(DOWN_ORDER):
                        wait_sum(dve, n, q * 6 + (6 + 3 * half), q * 16 + (U_MLP + 8 + 4 * half + 4))
                        V.tensor_tensor(x1[:, c, cols], bank[4 * (1 - half) + c][:], x1[:, c, cols],
                                        ALU.add).then_inc(down_added, 1)
                        if last and half and n:
                            final(n - 1)
                    if last and half == 0:
                        before_roots(1)
                        dve.wait_ge(gfin_loaded, 16)
                        for n, c in enumerate(DOWN_ORDER):
                            dve.wait_ge(down_added, 4 + 3 * 2 * NC + (n + 1))
                            V.tensor_tensor(xn2[:, c, 0:512], x1[:, c, 0:512], gfin[:, 0:512],
                                            ALU.mult).then_inc(xg_ready, 1)

            with dve.Fori(0, 3) as q:
                quarter(q, last=False)
            quarter(3, last=True)
            final(NC - 1)

        @block.tensor
        def _(pe):
            T = nc.tensor

            def unit(u, slot, read=None, landing=None):
                pe.wait_ge(whi_ready, u + 1)
                if read is not None:
                    pe.wait_ge(unit_read[slot], read)
                for k in range(KT):
                    if landing is not None:
                        pe.wait_ge(landing, k + 1)
                    for n, part in enumerate((h_hi, h_lo)):
                        T.matmul(bank[slot][:], whi[slot][:, k * P:(k + 1) * P], part[:, k, :],
                                 start=(k == 0 and n == 0), stop=False)
                pe.wait_ge(wlo_ready, u + 1)
                for k in range(KT):
                    mm = T.matmul(bank[slot][:], wlo[slot][:, k * P:(k + 1) * P], h_hi[:, k, :],
                                  start=False, stop=(k == KT - 1))
                mm.then_inc(unit_done, 1)

            pe.wait_ge(const_loaded, 16)
            for c in range(NC):
                if c == 2:
                    pe.wait_ge(rows_loaded, 16 * 7)
                    pe.wait_ge(small_loaded, 64)
                    T.transpose(bank[2][:, 0:P], rows1[:], ident)
                    T.transpose(bank[2][:, P:P + 96], rows2[:], ident[0:96, 0:96])
                    T.matmul(bank[2][:, 224:240], cst[0:2, K_HALF:K_HALF + P], d_two[:],
                             start=True, stop=True).then_inc(vec_turned, 1)
                pe.wait_ge(xn_ready, c + 1)
                for k in range(KT - 1):
                    mm = T.transpose(h_bank(k)[:, c * P:(c + 1) * P], xn[:, c, k * P:(k + 1) * P], ident)
                    if c == NC - 1:
                        mm.then_inc(xn_turned, 1)
            pe.wait_ge(vec_ready, 1)
            for c in range(NC):
                mm = T.transpose(h_bank(KT - 1)[:, c * P:(c + 1) * P], xn[:, c, D - P:D], ident)
            mm.then_inc(xn_turned, 1)
            unit(0, 0, landing=hlo_ready)
            unit(1, 1)

            def swap(src, bank_to, signal):
                T.matmul(bank_to[:], perm, src, start=True, stop=True).then_inc(signal, 1)

            def turn_v(b, pp):
                pe.wait_ge(unit_read[(U_KV + 4 * b + 6 + pp) % 2], (U_KV + 4 * b + 6 + pp) // 2 + 1)
                if b:
                    pe.wait_ge(v_ready, pp + 1)
                elif pp == 0:
                    pe.wait_ge(gate_ready, 1)
                for c in range(NC):
                    mm = T.transpose(bank[4 + pp][:, c * P:(c + 1) * P], vtmp[:, pp, c * P:(c + 1) * P], ident)
                mm.then_inc(v_turned, 1)

            def swap_k(b, pp):
                pe.wait_ge(unit_read[(U_KV + 4 * b + 4 + pp) % 2], (U_KV + 4 * b + 4 + pp) // 2 + 1)
                if b:
                    pe.wait_ge(k_ready, pp + 1)
                swap(kT[:, b, pp, :], bank[6 + pp], k_swapped)

            def hidden(i):
                if i == 0:
                    pe.wait_ge(cmpw_loaded, 16 * 6)
                    pe.wait_ge(dec_ready, 1)
                for half in range(2):
                    for jj in range(16):
                        if half == 0:
                            pe.wait_ge(blk_ready, 16 * i + jj + 1)
                        mm = T.matmul(bank[2 + i][:, half * P:(half + 1) * P].rearrange("p (g k) -> p g k", k=32)[:, :, 0:CMP],
                                      w1c[:, i, jj, half * P:(half + 1) * P],
                                      blk[:, jj, 0:KVG * CMP].rearrange("p (g k) -> p g k", k=CMP),
                                      start=(jj == 0), stop=(jj == 15))
                mm.then_inc(hid_summed, 1)

            for j in range(12):
                u = U_KV + j
                unit(u, u % 2, u // 2)
                if j == 1:
                    pe.wait_ge(dt_ready, 2)
                    pe.wait_ge(vec_ready, 1)
                    for i, row in enumerate((1, 4)):
                        for c in range(NC):
                            n = (i * NC + c) * HEADS
                            mm = T.transpose(bank[2][:, n:n + HEADS], dtw[:, row, c * P:(c + 1) * P],
                                             ident[0:HEADS, 0:HEADS])
                    mm.then_inc(dt_turned, 1)
                if j == 2:
                    pe.wait_ge(unit_read[1], 1)
                    for c in range(NC):
                        mm = T.transpose(bank[4][:, c * 48:(c + 1) * 48], ag[:, c * P:(c + 1) * P],
                                         ident[0:48, 0:48])
                    mm.then_inc(ag_turned, 1)
                    pe.wait_ge(dtT_ready, 1)
                    pe.wait_ge(ones_set, 3)
                    dta = dtT[:, 1].rearrange("p c h -> p (c h)")
                    T.matmul(bank[3][:, 0:P], stri, dta, start=True, stop=True)
                    T.matmul(bank[3][:, P:2 * P], ones[:], dta, start=True, stop=True).then_inc(dec_summed, 1)
                if j in (5, 9):
                    hidden(j // 9)
                if j in (5, 6, 9, 10):
                    swap_k(j // 8, (j - 1) % 2)
                if j in (7, 8, 11):
                    turn_v(j // 10, (j - 1) % 2)
                if j == 7:
                    pe.wait_ge(hid_ready, 1)
                    for half in range(2):
                        mm = T.matmul(bank[2][:, 0:P], w2c[:, 0, half].rearrange("p e d -> p (e d)"),
                                      hid[:, 0, half].rearrange("p g k -> p (g k)"), start=(half == 0), stop=(half == 1))
                    mm.then_inc(kvc_summed, 1)
                if j == 11:
                    pe.wait_ge(hidr_ready, 1)
                    for g in range(KVG):
                        for half in range(2):
                            mm = T.matmul(bank[3][:, g * HD:(g + 2) * HD], hidr[:, half, g].rearrange("p e k -> p (e k)"),
                                          w2c[:, 1, half].rearrange("p e d -> p (e d)"),
                                          start=(half == 0), stop=(half == 1))
                    mm.then_inc(kvc_summed, 1)
            turn_v(1, 1)

            pe.wait_ge(v_ready, 4)

            with pe.Fori(0, 2) as rr:
                def q_unit(j):
                    if j < 2:
                        pe.wait_ge(unit_read[j], U_Q // 2)
                    else:
                        pe.wait_ge(q_copied, rr * 4 + (j - 1))
                    unit(rr * 4 + (U_Q + j), j % 2)

                def swap_q(j):
                    if j >= 2:
                        pe.wait_ge(q_ready, rr * 4 + (j - 1))
                    pe.wait_ge(q_copied, rr * 4 + (j + 1))
                    swap(q_s[:, j, :], bank[6 + j % 2], q_swapped)

                def cmp_scores(pp):
                    pe.wait_ge(q_copied, rr * 4 + (2 * pp + 2))
                    for i in range(NC):
                        for r2 in range(2):
                            n = (i * 2 + r2) * 64
                            w = min(P, S - n)
                            mm = T.matmul(bank[4 + pp][:, n:n + w], q_s[:, 2 * pp + r2, i * P:(i + 1) * P],
                                          kc[:, pp, 0:w], start=True, stop=True)
                    mm.then_inc(cs_ready, 1)

                def scores(n):
                    i, b = divmod(n, 16)
                    g, r2, br = b // 4, b // 2 % 2, b % 2
                    pp, e = divmod(g, 2)
                    if n in (0, 2, 8, 10):
                        pe.wait_ge(qlo_ready, rr * 8 + (4 * pp + 2 * r2 + 2))
                    if n >= 4:
                        pe.wait_ge(exp_ready, rr * 64 + (n - 3))
                    to = score_bank(n)
                    w = max(i + 1, 2) * P
                    for part in kk[br]:
                        T.matmul(to[:, 0:w], q_hl[:, 2 * (2 * pp + r2) + e, i * P:(i + 1) * P], part[:, g, 0:w],
                                 start=(part is kk[br][0]), stop=(part is kk[br][1]))
                    T.matmul(to[:, i * P:(i + 1) * P], ident_bf[:], causal_bf[:],
                             start=False, stop=True, skip_group_check=True).then_inc(s_ready, 1)

                def turn(n):
                    pe.wait_ge(prob_ready, rr * 64 + (n + 1))
                    if n >= 2:
                        pe.wait_ge(pT_ready, rr * 64 + (n - 1))
                        if cmp_turned(n - 2):
                            j, t = cmp_turned(n - 2)
                            pe.wait_ge(pcT_ready, rr * 8 + (2 * j + t + 1))
                    else:
                        pe.wait_ge(cs_read, rr * 4 + (2 * n + 2))
                    if cmp_turned(n):
                        j, t = cmp_turned(n)
                        pe.wait_ge(cp_ready, rr * NC + (j + 1))
                        T.transpose(bank[4 + n % 2][:, 3 * P:S],
                                    cp[:, 2, 4 * t:4 * t + 4, :].rearrange("p h k -> p (h k)"), ident).then_inc(cp_turned, 1)
                    for t in range(n // 16 + 1):
                        mm = T.transpose(bank[4 + n % 2][:, t * P:(t + 1) * P], prob[n % 4][:, t * P:(t + 1) * P], ident)
                    mm.then_inc(prob_turned, 1)

                def weigh(n):
                    i, b = divmod(n, 16)
                    g, r2, br = b // 4, b // 2 % 2, b % 2
                    def to(half):
                        return bank[6 + g % 2][half * HD:(half + 1) * HD, 0:P]

                    if b % 4 == 0 and n >= 8:
                        pe.wait_ge(olo_ready, rr * 16 + (n // 4 - 1))
                    if n in (0, 4):
                        pe.wait_ge(q_ready, rr * 4 + (3 + n // 4))
                    if b % 4 == 3:
                        t = g % 2
                        pe.wait_ge(pcT_ready, rr * 8 + (2 * i + t + 1))
                        for half in range(2):
                            m = g // 2 * 2 + half
                            rows = slice(32 * m, 32 * m + 32)
                            T.matmul(to(half), vc[rows, g, :], pcT[i % 2][rows, t, :], start=False, stop=(half == 0))
                    pe.wait_ge(pT_ready, rr * 64 + (n + 1))
                    for t in range(i + 1):
                        mm = T.matmul(to(r2), vtok[:, br, t, g * HD:(g + 1) * HD], pT[n % 2][:, t * P:(t + 1) * P],
                                      start=(br == 0 and t == 0), stop=(b % 4 == 3 and t == i))
                    mm.then_inc(pv_done, 1)

                q_unit(0)
                q_unit(1)
                swap_q(0)
                q_unit(2)
                swap_q(1)
                pe.wait_ge(kvc_ready, 3)
                cmp_scores(0)
                q_unit(3)
                swap_q(2)
                pe.wait_ge(kklo_ready, 8)
                scores(0)
                scores(1)
                scores(2)
                cmp_scores(1)
                for n in range(64):
                    if n + 3 < 64:
                        scores(n + 3)
                    turn(n)
                    if n == 0:
                        swap_q(3)
                    if n:
                        weigh(n - 1)
                weigh(63)
                pe.wait_ge(olo_ready, rr * 16 + 16)

            def from_state(g):
                pe.wait_ge(prev_ready, g * 3 + 3)
                for j in range(2):
                    for c in range(1, NC):
                        mm = T.matmul(bank[4 + j][:, c * P:(c + 1) * P], prev[:, c - 1, j * P:(j + 1) * P],
                                      grp[:, 3, c * P:(c + 1) * P], start=True, stop=True)
                    mm.then_inc(yo_done, 1)

            def norm_sum(g, sums=2):
                for j in range(2):
                    pe.wait_ge(ysq_ready, g * 2 + (j + 1))
                    mm = T.matmul(bank[sums][:], mean_ssm[:], sq[:, j, :], start=(j == 0), stop=(j == 1))
                mm.then_inc(yms_done, 1)

            def group(g, first):
                def group_unit(j):
                    if j < 2:
                        pe.wait_ge(unit_read[j], g + Z_READ - 1)
                    else:
                        pe.wait_ge(conv_summed, g * 4 + (j - 1))
                    unit(g * 6 + (U_SSM + j), j % 2)

                def seg(c):
                    pe.wait_ge(segr_ready, g * 8 + (2 * c + 2))
                    if c >= 2:
                        pe.wait_ge(dec_exp, g * 4 + (c - 1))
                    elif not first:
                        pe.wait_ge(eo_ready, g * 2 - 1 + c)
                    for part in (seg_hi, seg_lo):
                        mm = T.matmul(bank[6 + c % 2][:], stri_r[:], part[:].rearrange("p h l -> p (h l)"),
                                      start=(part is seg_hi), stop=(part is seg_lo))
                    mm.then_inc(seg_summed, 1)

                group_unit(0)
                if not first:
                    from_state(g - 1)
                seg(0)
                for j in range(1, 4):
                    group_unit(j)
                    if j == 1 and not first:
                        norm_sum(g - 1)
                    seg(j)
                group_unit(4)
                if not first:
                    pe.wait_ge(yrs_ready, g)
                pe.wait_ge(conv_ready, g * 4 + 2)
                for n in range(2):
                    for c in range(2 * n, 2 * n + 2):
                        for j in range(2):
                            mm = T.transpose(bank[2 + n][:, (c % 2) * 256 + j * P:(c % 2) * 256 + (j + 1) * P],
                                             grp[:, j, c * P:(c + 1) * P], ident)
                    mm.then_inc(x_turned, 1)
                pe.wait_ge(conv_ready, g * 4 + 3)
                for c in range(NC):
                    mm = T.transpose(bank[4][:, c * P:(c + 1) * P], grp[:, 2, c * P:(c + 1) * P], ident)
                mm.then_inc(b_turned, 1)
                pe.wait_ge(conv_ready, g * 4 + 4)
                for c in range(NC):
                    tok = slice(c * P, (c + 1) * P)
                    mm = T.matmul(bank[5][:, tok], grp[:, 2, tok], grp[:, 3, tok], start=True, stop=True)
                mm.then_inc(cb_done, 1)
                group_unit(5)
                pe.wait_ge(xdd_ready, g * 2 + 2)
                pe.wait_ge(btok_ready, g + 1)
                pe.wait_ge(cbm_ready, g + 1)
                for c in range(NC - 1):
                    mm = T.matmul(bank[4 + c // 2][:, (c % 2) * 256:(c % 2) * 256 + 256], btok[:, c, :], xdd[:, c, :],
                                  start=True, stop=True)
                mm.then_inc(st_done, 1)
                pe.wait_ge(mdec_ready, g * 4 + 4)
                for j in range(2):
                    for c in range(NC):
                        for e in range(2):
                            h = 2 * j + e
                            mm = T.matmul(bank[2 + j][e * HD:(e + 1) * HD, c * P:(c + 1) * P],
                                          xdt[:, c, h * HD:(h + 1) * HD], mdec[:, c, h, :], start=True, stop=True)
                    mm.then_inc(yd_done, 1)
                for j in range(2):
                    for c in range(1, NC):
                        mm = T.matmul(bank[6 + j][:, c * P:(c + 1) * P], dtab[:, c - 1, j * P:(j + 1) * P], tri,
                                      start=True, stop=True)
                    mm.then_inc(eo_summed, 1)
            group(0, first=True)
            with pe.Fori(1, GROUPS) as g:
                group(g, first=False)

            def product(u, slot, to, hi, lo, k0, start, stop, landing=None):
                pe.wait_ge(whi_ready, u + 1)
                for k in range(KT):
                    if landing is not None:
                        pe.wait_ge(landing, k + 1)
                    for n, part in enumerate((hi, lo)):
                        T.matmul(to[:], whi[slot][:, k * P:(k + 1) * P], part[:, k0 + k, :],
                                 start=(start and k == 0 and n == 0), stop=False)
                pe.wait_ge(wlo_ready, u + 1)
                for k in range(KT):
                    mm = T.matmul(to[:], wlo[slot][:, k * P:(k + 1) * P], hi[:, k0 + k, :],
                                  start=False, stop=(stop and k == KT - 1))
                mm.then_inc(unit_done, 1)

            def product_rows(u, slot, banks, hi, lo, kb, order):
                def high(c):
                    for k in range(2):
                        for n, part in enumerate((hi, lo)):
                            T.matmul(banks[c][:], part[:, 2 * kb + k, c * P:(c + 1) * P],
                                     whi[slot][:, k * 512:(k + 1) * 512],
                                     start=(kb == 0 and k == 0 and n == 0), stop=False)

                def low(c):
                    for k in range(2):
                        mm = T.matmul(banks[c][:], hi[:, 2 * kb + k, c * P:(c + 1) * P],
                                      wlo[slot][:, k * 512:(k + 1) * 512], start=False, stop=(kb == 3 and k == 1))
                    return mm

                pe.wait_ge(whi_ready, u + 1)
                if kb < 3:
                    for c in order:
                        high(c)
                    pe.wait_ge(wlo_ready, u + 1)
                    for c in order:
                        mm = low(c)
                else:
                    pe.wait_ge(wlo_ready, u + 1)
                    for c in order:
                        high(c)
                        mm = low(c)
                        if c != order[-1]:
                            mm.then_inc(sum_done, 1)
                mm.then_inc(unit_done, 1)

            def mix(m, first):
                for t in range(2):
                    pe.wait_ge(mlo_ready, m * 2 + (t + 1))
                    for i, (hi, lo, k0, start, stop) in enumerate((
                            (h_hi, h_lo, 0, True, True), (h_hi, h_lo, 0, True, True), (o_hi, o_lo, 0, True, True),
                            (y_hi, y_lo, 0, True, False), (y_hi, y_lo, KT, False, True))):
                        j = 5 * t + i
                        if first and j in (3, 4):
                            pe.wait_ge(ylo_ready, GROUPS if j == 3 else 2 * GROUPS)
                        product(m * 10 + (U_MIX + j), j % 2, bank[4 * t + min(i, 3)], hi, lo, k0, start, stop)
                        if first and j == 0:
                            from_state(GROUPS - 1)
                        if first and j == 1:
                            pe.wait_ge(eo_ready, 2 * GROUPS)
                            norm_sum(GROUPS - 1, sums=6)

            pe.wait_ge(unit_read[0], U_Q // 2 + GROUPS)
            pe.wait_ge(unit_read[1], U_Q // 2 + GROUPS)
            mix(0, first=True)
            with pe.Fori(1, 4) as m:
                mix(m, first=False)

            for j in range(8):
                half, kb = divmod(j, 4)
                if kb == 3 and half == 0:
                    pe.wait_ge(mlo_ready, KT + 2)
                elif kb == 0 and half == 0:
                    pe.wait_ge(mlo_ready, KT + 1)
                product_rows(U_WO + j, j % 2, bank[4 * half:4 * half + 4], m_hi, m_lo, kb, WO_ORDER)

            def turn_h2(k, c):
                return T.transpose(h2_bank(k)[:, c * P:(c + 1) * P], xn2[:, c, k * P:(k + 1) * P], ident)

            for n, c in enumerate(WO_ORDER):
                pe.wait_ge(xn2_first, n + 1)
                for k in range(KT // 2):
                    mm = turn_h2(k, c)
                    if n == NC - 1:
                        mm.then_inc(xn2_turned, 1)
            pe.wait_ge(xn2_ready, NC)
            for k in range(KT // 2, KT):
                for c in range(NC):
                    mm = turn_h2(k, c)
                mm.then_inc(xn2_turned, 1)

            with pe.Fori(0, 4) as q:
                for j in range(8):
                    if j >= 2:
                        pe.wait_ge(relu_ready, q * 8 + (j - 1))
                    else:
                        pe.wait_ge(down_added, q * 8 + (j + 1))
                    product(q * 16 + (U_MLP + j), j % 2, bank[2 + j % 2], h_hi, h_lo, 0, True, True,
                            landing=h2lo_ready if j == 0 else None)
                for j in range(8):
                    half, kb = divmod(j, 4)
                    if kb == 0 and half == 1:
                        pe.wait_ge(relu_ready, q * 8 + 8)
                        pe.wait_ge(down_added, q * 8 + 4)
                    pe.wait_ge(ulo_ready, q * 8 + (2 * kb + 2))
                    product_rows(q * 16 + (U_MLP + 8 + j), j % 2, bank[4 * (1 - half):4 * (1 - half) + 4],
                                 u_hi, u_lo, kb, DOWN_ORDER)

def kernel(**inputs):
    import numpy as _np
    import concourse.bacc as _bacc
    from concourse import mybir as _mybir
    from concourse.bass_utils import run_bass_kernel_spmd as _run

    nc = _bacc.Bacc("TRN2", target_bir_lowering=False, num_devices=1)
    arrays, args = {}, {}
    inputs = dict(inputs, consts=shape_constants())
    for name, value in inputs.items():
        v = _np.ascontiguousarray(value)
        arrays[f"in_{name}"] = v
        args[name] = nc.dram_tensor(f"in_{name}", v.shape, _mybir.dt.from_np(v.dtype), kind="ExternalInput").ap()
    out = nc.dram_tensor("out", (1, S, D), F32, kind="ExternalOutput").ap()
    build(nc, args, out)
    r = _run(nc, [arrays], core_ids=[0])
    return r.results[0]["out"]
```
